# Optimizing a Trainium2 kernel written in Bass

```python
import jax, jax.numpy as jnp
from jax import lax
import numpy as np

D_MODEL = 1024
BATCH = 1
SEQ = 128
DEPTH = 1
DEC_BATCH = 1
DEC_SEQ = 512
PAST_LEN = 128

GRID_W = 64
N_HEADS = 8
QK_NOPE = 64
QK_ROPE = 32
V_HEAD = 64
Q_LORA = 256
KV_LORA = 128
ROPE_AXIS = QK_ROPE // 2
ROPE_BASE = 10000.0
ATTN_SCALE = (QK_NOPE + QK_ROPE) ** -0.5
Q_BLOCK = 128
D_CONV = D_MODEL
CONV_W = 3
N_GROUPS = 4
EXP_PER_GROUP = 8
N_EXPERTS = N_GROUPS * EXP_PER_GROUP
TOP_K = 2
D_EXPERT = 256
EPS = 1e-6
IN_COLS = 3 * D_CONV + Q_LORA + KV_LORA + QK_ROPE + 2 * D_MODEL

kernel_name = "hybrid_dit_conv_mla_hmoe_step"

def rmsnorm(x, g):
    xf = x.astype(jnp.float32)
    r = lax.rsqrt(jnp.mean(xf * xf, axis=-1, keepdims=True) + EPS)
    return (xf * r).astype(x.dtype) * g

def axial_rope_tables(n_tokens):
    rows = n_tokens // GRID_W
    row = jnp.repeat(jnp.arange(rows), GRID_W).astype(jnp.float32)
    col = jnp.tile(jnp.arange(GRID_W), rows).astype(jnp.float32)
    inv = 1.0 / (ROPE_BASE ** (jnp.arange(0, ROPE_AXIS, 2, dtype=jnp.float32) / ROPE_AXIS))
    ang = jnp.stack([row[:, None] * inv, col[:, None] * inv], axis=1)
    return jnp.cos(ang), jnp.sin(ang)

def apply_axial_rope(x, cos, sin):
    shp = x.shape
    half = ROPE_AXIS // 2
    xr = x.reshape(shp[:-1] + (2, 2, half))
    x1, x2 = xr[..., 0, :], xr[..., 1, :]
    bshape = (shp[1],) + (1,) * (x.ndim - 3) + (2, half)
    cs = cos.reshape(bshape).astype(x.dtype)
    sn = sin.reshape(bshape).astype(x.dtype)
    out = jnp.stack([x1 * cs - x2 * sn, x2 * cs + x1 * sn], axis=-2)
    return out.reshape(shp)

def attend(q_nope, q_rope, k_nope, k_rope, v):
    b, n = q_nope.shape[0], q_nope.shape[1]
    nb = n // Q_BLOCK
    qn = jnp.moveaxis(q_nope.reshape(b, nb, Q_BLOCK, N_HEADS, QK_NOPE), 1, 0)
    qr = jnp.moveaxis(q_rope.reshape(b, nb, Q_BLOCK, N_HEADS, QK_ROPE), 1, 0)

    def block(args):
        qn_b, qr_b = args
        s = (jnp.einsum('bqhd,bkhd->bhqk', qn_b, k_nope)
             + jnp.einsum('bqhr,bkr->bhqk', qr_b, k_rope)) * ATTN_SCALE
        p = jax.nn.softmax(s.astype(jnp.float32), axis=-1).astype(v.dtype)
        return jnp.einsum('bhqk,bkhd->bqhd', p, v)

    o = lax.map(block, (qn, qr))
    return jnp.moveaxis(o, 0, 1).reshape(b, n, N_HEADS * V_HEAD)

def mixer(h, lw, rope, ctx_ckv, ctx_krope):
    b, n, _ = h.shape
    proj = h @ lw['w_in']
    sizes = [D_CONV, D_CONV, D_CONV, Q_LORA, KV_LORA, QK_ROPE, D_MODEL, D_MODEL]
    idx = [int(s) for s in np.cumsum(sizes)[:-1]]
    bg, cg, u_in, cq_raw, ckv_raw, kr, g_conv, g_mla = jnp.split(proj, idx, axis=-1)
    u = jnp.pad(cg * u_in, ((0, 0), (1, 1), (0, 0)))
    w = lw['conv_w']
    conv = u[:, :-2] * w[0] + u[:, 1:-1] * w[1] + u[:, 2:] * w[2]
    y_conv = (bg * conv) @ lw['w_conv_out']
    q = (rmsnorm(cq_raw, lw['q_norm']) @ lw['w_uq']).reshape(b, n, N_HEADS, QK_NOPE + QK_ROPE)
    q_nope, q_rope = q[..., :QK_NOPE], q[..., QK_NOPE:]
    ckv = rmsnorm(ckv_raw, lw['kv_norm'])
    if rope is not None:
        q_rope = apply_axial_rope(q_rope, rope[0], rope[1])
        kr = apply_axial_rope(kr, rope[0], rope[1])
    if ctx_ckv is not None:
        ckv_all = jnp.concatenate([ckv, ctx_ckv.astype(ckv.dtype)], axis=1)
        kr_all = jnp.concatenate([kr, ctx_krope.astype(kr.dtype)], axis=1)
    else:
        ckv_all, kr_all = ckv, kr
    m = ckv_all.shape[1]
    kv = (ckv_all @ lw['w_ukv']).reshape(b, m, N_HEADS, QK_NOPE + V_HEAD)
    k_nope, v_h = kv[..., :QK_NOPE], kv[..., QK_NOPE:]
    y_mla = attend(q_nope, q_rope, k_nope, kr_all, v_h) @ lw['w_o']
    merged = jax.nn.sigmoid(g_conv) * y_conv + jax.nn.sigmoid(g_mla) * y_mla
    return merged @ lw['w_mix_out'], ckv, kr

def hier_moe(h, lw):
    shp = h.shape
    t = h.reshape(-1, D_MODEL)
    p_grp = jax.nn.softmax((t @ lw['w_grp']).astype(jnp.float32), axis=-1)
    p_g, g_idx = lax.top_k(p_grp, 1)
    e_logits = (t @ lw['w_exp']).astype(jnp.float32).reshape(-1, N_GROUPS, EXP_PER_GROUP)
    sel = jnp.take_along_axis(e_logits, g_idx[:, :, None], axis=1)[:, 0]
    p_e = jax.nn.softmax(sel, axis=-1)
    top_w, top_i = lax.top_k(p_e, TOP_K)
    top_w = p_g * top_w / jnp.sum(top_w, axis=-1, keepdims=True)
    glob = g_idx * EXP_PER_GROUP + top_i
    combine = jnp.sum(jax.nn.one_hot(glob, N_EXPERTS, dtype=jnp.float32) * top_w[..., None], axis=1)
    combine = combine.astype(h.dtype)
    a = jnp.einsum('td,edf->tef', t, lw['w_up'])
    g = jnp.einsum('td,edf->tef', t, lw['w_gate'])
    act = jax.nn.silu(g) * a * combine[:, :, None]
    out = jnp.einsum('tef,efd->td', act, lw['w_down'])
    return out.reshape(shp)

def block(x, cond, lw, rope, ctx_ckv, ctx_krope):
    mod = jax.nn.silu(cond) @ lw['w_ada'] + lw['b_ada']
    shift1, scale1, gate1, shift2, scale2, gate2 = jnp.split(mod, 6, axis=-1)
    h = rmsnorm(x, lw['norm1']) * (1 + scale1) + shift1
    y, ckv, kr = mixer(h, lw, rope, ctx_ckv, ctx_krope)
    x = x + gate1 * y
    h = rmsnorm(x, lw['norm2']) * (1 + scale2) + shift2
    x = x + gate2 * hier_moe(h, lw)
    return x, ckv, kr

def setup_inputs(seed: int = 0) -> dict:
    key = jax.random.key(seed)
    ks = jax.random.split(key, 32)
    f32 = jnp.float32

    def nrm(k, shape, scale):
        return jax.random.normal(k, shape, f32) * scale

    def gain(k, shape):
        return 1.0 + 0.05 * jax.random.normal(k, shape, f32)

    L = DEPTH
    return {
        'x_prompt': nrm(ks[0], (BATCH, SEQ, D_MODEL), 1.0),
        'x_sample': nrm(ks[1], (DEC_BATCH, DEC_SEQ, D_MODEL), 1.0),
        'cache_ckv': nrm(ks[2], (DEC_BATCH, DEPTH, PAST_LEN, KV_LORA), 1.0),
        'cache_krope': nrm(ks[3], (DEC_BATCH, DEPTH, PAST_LEN, QK_ROPE), 1.0),
        'c': nrm(ks[4], (DEC_BATCH, D_MODEL), 1.0),
        'c_ctx': nrm(ks[5], (D_MODEL,), 1.0),
        'norm1': gain(ks[6], (L, D_MODEL)),
        'w_ada': nrm(ks[7], (L, D_MODEL, 6 * D_MODEL), D_MODEL ** -0.5),
        'b_ada': nrm(ks[8], (L, 6 * D_MODEL), 0.02),
        'w_in': nrm(ks[9], (L, D_MODEL, IN_COLS), D_MODEL ** -0.5),
        'conv_w': nrm(ks[10], (L, CONV_W, D_CONV), CONV_W ** -0.5),
        'w_conv_out': nrm(ks[11], (L, D_CONV, D_MODEL), D_CONV ** -0.5),
        'q_norm': gain(ks[12], (L, Q_LORA)),
        'w_uq': nrm(ks[13], (L, Q_LORA, N_HEADS * (QK_NOPE + QK_ROPE)), Q_LORA ** -0.5),
        'kv_norm': gain(ks[14], (L, KV_LORA)),
        'w_ukv': nrm(ks[15], (L, KV_LORA, N_HEADS * (QK_NOPE + V_HEAD)), KV_LORA ** -0.5),
        'w_o': nrm(ks[16], (L, N_HEADS * V_HEAD, D_MODEL), (N_HEADS * V_HEAD) ** -0.5),
        'w_mix_out': nrm(ks[17], (L, D_MODEL, D_MODEL), D_MODEL ** -0.5),
        'norm2': gain(ks[18], (L, D_MODEL)),
        'w_grp': nrm(ks[19], (L, D_MODEL, N_GROUPS), D_MODEL ** -0.5),
        'w_exp': nrm(ks[20], (L, D_MODEL, N_EXPERTS), D_MODEL ** -0.5),
        'w_up': nrm(ks[21], (L, N_EXPERTS, D_MODEL, D_EXPERT), D_MODEL ** -0.5),
        'w_gate': nrm(ks[22], (L, N_EXPERTS, D_MODEL, D_EXPERT), D_MODEL ** -0.5),
        'w_down': nrm(ks[23], (L, N_EXPERTS, D_EXPERT, D_MODEL), D_EXPERT ** -0.5),
        'final_norm': gain(ks[24], (D_MODEL,)),
    }

def reference(x_prompt, x_sample, cache_ckv, cache_krope, c, c_ctx, norm1, w_ada, b_ada,
              w_in, conv_w, w_conv_out, q_norm, w_uq, kv_norm, w_ukv, w_o, w_mix_out,
              norm2, w_grp, w_exp, w_up, w_gate, w_down, final_norm):
    rope = axial_rope_tables(x_sample.shape[1])
    xp, xs = x_prompt, x_sample
    ckv_states, krope_states = [], []
    for l in range(DEPTH):
        lw = {
            'norm1': norm1[l], 'w_ada': w_ada[l], 'b_ada': b_ada[l], 'w_in': w_in[l],
            'conv_w': conv_w[l], 'w_conv_out': w_conv_out[l], 'q_norm': q_norm[l],
            'w_uq': w_uq[l], 'kv_norm': kv_norm[l], 'w_ukv': w_ukv[l], 'w_o': w_o[l],
            'w_mix_out': w_mix_out[l], 'norm2': norm2[l], 'w_grp': w_grp[l],
            'w_exp': w_exp[l], 'w_up': w_up[l], 'w_gate': w_gate[l], 'w_down': w_down[l],
        }
        xp, ckv_p, kr_p = block(xp, c_ctx, lw, None, None, None)
        ckv_states.append(ckv_p)
        krope_states.append(kr_p)
        xs, _, _ = block(xs, c[:, None, :], lw, rope, cache_ckv[:, l], cache_krope[:, l])
    y_prompt = rmsnorm(xp, final_norm)
    y_sample = rmsnorm(xs, final_norm)
    new_ckv = jnp.stack(ckv_states, axis=1)
    new_krope = jnp.stack(krope_states, axis=1)
    return (y_prompt, y_sample, new_ckv, new_krope)


_drawn_inputs = setup_inputs


def setup_inputs(seed=0):
    import zlib

    import numpy as np

    out = dict(_drawn_inputs(seed))
    spreads = {}
    factors = {'cache_ckv': 3.464, 'cache_krope': 5.759, 'q_norm': 8.0}
    for name, (base, spread) in spreads.items():
        noise = np.random.default_rng([zlib.crc32(name.encode()), seed]).standard_normal(out[name].shape)
        drawn = base * np.exp(spread * noise) if base else spread * noise
        out[name] = __import__('jax').numpy.asarray(drawn.astype(out[name].dtype))
    for name, factor in factors.items():
        out[name] = (out[name] * factor).astype(out[name].dtype)
    return out
```

```python
from contextlib import ExitStack

import numpy as np

import concourse.bass as bass
from concourse import mybir

ALU = mybir.AluOpType
ACT = mybir.ActivationFunctionType
AXX = mybir.AxisListType.X
F32 = mybir.dt.float32
F32R = mybir.dt.float32r
BF16 = mybir.dt.bfloat16
U32 = mybir.dt.uint32
I32 = mybir.dt.int32

P = 128
D = 1024
KD = D // P
N_SAMPLE, N_PROMPT, N_PAST = 512, 128, 128
T = N_SAMPLE + N_PROMPT
NT = T // P
NTS = N_SAMPLE // P
HALF = T // 2
NH, NOPE, ROPE, VH = 8, 64, 32, 64
QK = NOPE + ROPE
QL, KVL = 256, 128
LAT = QL + KVL + ROPE
KEYS = N_SAMPLE + N_PAST
NKT = KEYS // P
ALLK = KEYS + N_PROMPT
SCALE = float(QK) ** -0.5
GRID_W = 64
NG, EPG = 4, 8
NE = NG * EPG
DE = 256
EPS = 1e-6
PIECE = 2048
C_BG, C_CG, C_U, C_LAT = 0, D, 2 * D, 3 * D
C_GC = C_LAT + LAT
C_GM = C_GC + D
FAR = 1 << 16
BIG = 1e30
X_MAX = 2 * ((2 * T // P - 1 + 1) // 2)
N_LIST = (NE + X_MAX + 4) * P

K_ID, K_TRI, K_ONE = 0, 128, 256
K_SEL = 384
K_COS, K_SIN = 640, 704
K_IOTA = 768
K_REV = 800
K_TOK = 832
K_DST = 837
K_N = 848


def constants():
    c = np.zeros((P, K_N), np.float32)
    c[:, K_ID:K_ID + P] = np.eye(P)
    c[:, K_TRI:K_TRI + P] = np.triu(np.ones((P, P)), 1)
    c[:, K_ONE:K_ONE + P] = 1
    for s in range(2):
        c[[s, 2 + s, 4], K_SEL + s * P:K_SEL + (s + 1) * P] = 1
    inv = 1.0 / (np.float32(10000.0) ** (np.arange(0, 16, 2, dtype=np.float32) / np.float32(16)))
    tok = np.arange(N_SAMPLE)
    ang = np.stack([(tok // GRID_W).astype(np.float32)[:, None] * inv,
                    (tok % GRID_W).astype(np.float32)[:, None] * inv], 1).astype(np.float32)
    for k, f in ((K_COS, np.cos), (K_SIN, np.sin)):
        c[:, k:k + 64] = f(ang).reshape(NTS, P, 16).transpose(1, 0, 2).reshape(P, 64)
    c[:, K_IOTA:K_IOTA + NE] = np.arange(NE)
    c[:, K_REV:K_REV + NE] = NE - np.arange(NE)
    t = np.arange(P)[:, None] + P * np.arange(NT)
    bits = np.zeros((P, 15), np.uint32)
    bits[:, 0:5] = t
    bits[:, 5:15] = (2 * t[:, :, None] + np.arange(2)).reshape(P, 10)
    c[:, K_TOK:K_TOK + 15] = bits.view(np.float32)
    return c


def build(nc, io):
    es = ExitStack()

    def sem(name):
        return es.enter_context(nc.semaphore(name))

    def sb(name, shape, dt=F32, scope=None):
        return (scope or es).enter_context(nc.sbuf_tensor(name, shape, dt))

    H2D = nc.dram_tensor("h2_rows", [T, D], F32, kind="Internal").ap()
    YD = nc.dram_tensor("expert_rows", [2 * T, D], F32, kind="Internal").ap()
    MODD = nc.dram_tensor("mod_parts", [4, 6 * D], F32, kind="Internal").ap()
    LISTD = nc.dram_tensor("slot_list", [N_LIST, 4], F32, kind="Internal").ap()

    cst = sb("cst", [P, K_N])
    ident = cst[:, K_ID:K_ID + P]
    vT = sb("vT", [P, 48])
    shsc = sb("shsc", [P, 16, 2])
    gain1 = sb("gain1", [P, KD, 2])
    stat = sb("stat", [P, 96])
    cond4 = sb("cond4", [P, KD, 4], F32R)
    stg = [sb(f"stg{i}", [4, 256]) for i in range(2)]
    extra_i = sb("extra_i", [P, 1], I32)
    expert_i = sb("expert_i", [P, NE + X_MAX + 2], I32)
    rec_at = sb("rec_at", [P, NT, 2], U32)
    tri_b = sb("tri_b", [P, P], BF16)
    one_b = sb("one_b", [P, P], BF16)
    fill = sb("fill", [P, N_LIST * 4 // P])

    mixer = ExitStack()
    raw = [sb(f"raw{i}", [P, PIECE], scope=mixer) for i in range(4)]
    hi = [sb(f"hi{i}", [P, PIECE], F32R, scope=mixer) for i in range(2)]
    lo = [sb(f"lo{i}", [P, PIECE], F32R, scope=mixer) for i in range(2)]
    hT = [sb(f"hT{i}", [P, KD, T], F32R, scope=mixer) for i in range(2)]
    part0 = ExitStack()
    x_tok = sb("x_tok", [P, NT, D], scope=part0)
    xnT = sb("xnT", [P, KD, T], scope=part0)
    sq0 = sb("sq0", [P, D], scope=part0)
    mod1 = sb("mod1", [5, 2 * D], scope=part0)
    cond2 = sb("cond2", [P, KD, 2], scope=part0)
    vecs = sb("vecs", [48, P], scope=part0)
    part0.close()
    part1 = ExitStack()
    lat = sb("lat", [P, NT + 1, LAT], scope=part1)
    cqT = [sb(f"cqT{i}", [P, 2, T], F32R, scope=part1) for i in range(2)]
    ckvT = [sb(f"ckvT{i}", [P, ALLK], F32R, scope=part1) for i in range(2)]
    qtok = [sb(f"qtok{i}", [P, NH, QK], scope=part1) for i in range(2)]
    rt = [sb(f"rt{i}", [P, NH, 2, 8], scope=part1) for i in range(4)]
    part1.close()
    oT = [sb(f"oT{i}", [P, 4, T], F32R, scope=mixer) for i in range(2)]
    part2 = ExitStack()
    prob = [sb(f"prob{i}", [P, KEYS], scope=part2) for i in range(2)]
    pT = sb("pT", [P, NKT, N_SAMPLE], scope=part2)
    qT = sb("qT", [QK, NH, T], scope=part2)
    kT = sb("kT", [QK, NH, ALLK], scope=part2)
    V = sb("V", [P, NKT + 1, NH * VH], scope=part2)
    qn_b = sb("qn_b", [P, QL], scope=part2)
    kvn_b = sb("kvn_b", [P, KVL], scope=part2)
    part2.close()
    part3 = ExitStack()
    cT = [sb(f"cT{i}", [P, KD, T], F32R, scope=part3) for i in range(2)]
    part3c = ExitStack()
    cg_s = [sb(f"cg_s{i}", [P, T], scope=part3c) for i in range(2)]
    u = [sb(f"u{i}", [P, T + 4], scope=part3c) for i in range(2)]
    cv = [sb(f"cv{i}", [P, T + 2], scope=part3c) for i in range(2)]
    stg_c = sb("stg_c", [4, 4 * 256], scope=part3c)
    part3c.close()
    merged = sb("merged", [P, KD, T], scope=part3)
    sg = [sb(f"sg{i}", [P, T], scope=part3) for i in range(2)]
    part3.close()
    mixer.close()

    p6 = ExitStack()
    h2T = sb("h2T", [P, KD, T], scope=p6)
    h2s = [sb(f"h2s{i}", [P, D], scope=p6) for i in range(2)]
    gain2 = sb("gain2", [P, 2, D], scope=p6)
    shift2 = sb("shift2", [P, 2, D], scope=p6)
    p6.close()
    xg = [sb(f"xg{i}", [P, D]) for i in range(2)]
    xgT = [[sb(f"xgT{i}{h}", [P, KD, P], F32R) for h in range(2)] for i in range(2)]
    yo = [sb(f"yo{i}", [P, D]) for i in range(2)]
    actT = [sb(f"actT{h}", [P, 2, P], F32R) for h in range(2)]
    sa = [sb(f"sa{i}", [P, DE]) for i in range(2)]
    act_v = [sb(f"act_v{i}", [P, DE]) for i in range(2)]
    lst_g = [sb(f"lst_g{i}", [P, 4]) for i in range(2)]
    lst_s = [sb(f"lst_s{i}", [P, 4]) for i in range(2)]
    pad0 = sb("pad0", [P, 1500])
    lg36 = sb("lg36", [NG + NE, T])
    wrt = sb("wrt", [P, KD, NG + NE])
    lg = sb("lg", [P, NT, NG + NE])
    hot = [sb(f"hot{i}", [P, NT, NE]) for i in range(2)]
    mask = sb("mask", [P, NT, NE], BF16)
    r_t = sb("r_t", [P, NT, NE])
    r_gs, r_ge, r_gh = (sb(f"r_g{i}", [P, NT, NG]) for i in range(3))
    r5 = [sb(f"r5_{i}", [P, NT]) for i in range(8)]
    r1 = sb("r1", [P, 4])
    r_x = [sb(f"r_x{i}", [P, NE]) for i in range(5)]
    r_e = sb("r_e", [P, X_MAX])
    rec = sb("rec", [P, NT, 2, 4])
    wh = [sb(f"wh{i}", [P, PIECE], F32R) for i in range(3)]
    wl = [sb(f"wl{i}", [P, PIECE], F32R) for i in range(3)]
    gate2 = sb("gate2", [P, 2, D])
    norm2_b = sb("norm2_b", [P, D])

    x1 = sb("x1", [P, NT, D])
    gate1 = sb("gate1", [P, 2, D])
    p7 = ExitStack()
    early = ExitStack()
    modt = sb("modt", [5, 4 * D], scope=early)
    early.close()
    wr = [[sb(f"wraw{k}{i}", [P, PIECE], scope=p7) for i in range(2)] for k in (2, 0, 1)]
    wr = wr[1:] + wr[:1]
    p7.close()
    p8 = ExitStack()
    ya = [sb(f"ya{i}", [P, 2, D], scope=p8) for i in range(2)]
    yt = [sb(f"yt{i}", [P, D], scope=p8) for i in range(2)]
    fn_b = sb("fn_b", [P, D], scope=p8)
    p8.close()

    bank = [es.enter_context(nc.psum_tensor(f"bank{i}", [P, 512], F32)) for i in range(8)]

    s_cst, s_vec, s_bc, s_cache, s_mod1, s_modt, s_n2, s_fn = (sem(n) for n in (
        "cst_in", "vec_in", "norms_in", "cache_in", "mod1_in", "modt_in", "norm2_in", "fnorm_in"))
    x_in = [sem(f"x_in{i}") for i in range(NT)]
    x_again = [sem(f"x_again{i}") for i in range(NT)]
    raw_in = [sem(f"raw_in{i}") for i in range(4)]
    hi_done, lo_done, piece_used = sem("hi_done"), sem("lo_done"), sem("piece_used")
    dchain, achain = sem("dve_chain"), sem("act_chain")
    s_ukv_v = sem("w_ukv_v_in")
    s_vT, c_vT, s_cond2, s_cond = sem("vT_ps"), sem("vT_sb"), sem("cond2"), sem("cond4_rdy")
    stg_ready = sem("stg_ready")
    mod_w = [sem(f"mod_w{i}") for i in range(2)]
    s_rms0, s_xn, s_xT, s_xTe = sem("rms0"), sem("xn"), sem("xT_ps"), sem("xT_sb")
    s_m1T, s_aff, s_hhi, s_hlo = sem("mod1T_ps"), sem("h_affine"), sem("h_hi"), sem("h_lo")
    s_lat, s_rmsl, s_latn, s_lT, s_lTh, s_lTe = (sem(n) for n in (
        "lat_ps", "rms_lat", "lat_norm", "latT_ps", "latT_hi", "latT_sb"))
    s_q, s_qr, s_tq, s_tqe, s_kv, s_kve = (sem(n) for n in (
        "q_ps", "q_roped", "qT_ps", "qT_sb", "kv_ps", "kv_sb"))
    s_sc, s_mx, s_ex, s_pn, s_tp, s_pe, s_pv, s_oh, s_ol = (sem(n) for n in (
        "scores", "neg_max", "exps", "probs", "pT_ps", "pT_sb", "pv", "o_hi", "o_lo"))
    blk_done, blk_free, mod_c = sem("conv_done"), sem("conv_free"), sem("mod_c")
    gate_done, gate_free, y_done, y_free = sem("gate_done"), sem("gate_free"), sem("y_done"), sem("y_free")
    s_mhi, s_mlo = sem("merged_hi"), sem("merged_lo")
    s_bcp, s_bce = sem("bcast_ps"), sem("bcast_sb")
    s_mix, s_mixe = sem("mix_ps"), sem("mix_sb")
    s_rms2, s_h2, s_h2T, s_h2Te = sem("rms2"), sem("h2_tok"), sem("h2T_ps"), sem("h2T_sb")
    h2_w = [sem(f"h2_w{i}") for i in range(2)]
    s_wr, s_lg, s_lgT = sem("router_w_in"), sem("logits_ps"), sem("logitsT_ps")
    s_lge, s_lgTe = sem("logits_sb"), sem("logitsT_sb")
    s_gx, s_dx, s_mask, s_pos = sem("grp_exp"), sem("top2_exp"), sem("mask_rdy"), sem("pos_ps")
    s_tri, s_fill, s_fillw = sem("tri_rdy"), sem("fill_rdy"), sem("fill_w")
    s_rec, s_scat, s_extra, s_gx_in, s_dx_in = (sem(n) for n in (
        "rec_rdy", "list_w", "extra_rdy", "grp_shift", "top2_diff"))
    s_latw = sem("lat_w")
    sp_turns, pool_turns = sem("sp_turns"), sem("pool_turns")

    w_done = [[sem(f"moe_{what}_{k}") for k in "abc"] for what in ("hi", "lo", "used")]
    wr_in = [[sem(f"moe_raw_{k}{i}") for i in range(2)] for k in "abc"]
    s_tr, s_xgh, s_xgl, s_si, s_act, s_at, s_aT, s_aTh, s_ya, s_yd, s_xg0 = (sem(n) for n in (
        "xgT_ps", "xgT_hi", "xgT_lo", "silu_up", "act_rdy", "actT_ps", "actT_sb", "actT_hi", "y_lower", "y_upper", "xg_zeroed"))
    lg_in, ls_in, gat, sct = ([sem(f"{n}{i}") for i in range(2)] for n in ("list_g", "list_s", "gathered", "scattered"))
    ya_in = [sem(f"ya_in{i}") for i in range(2)]
    y_out = [sem(f"y_out{i}") for i in range(2)]
    s_x2, s_sq3, s_rms3, s_yt = sem("x2_rdy"), sem("sq3"), sem("rms3"), sem("yt_rdy")

    def v3(t, k, c):
        return t[:, 0:k * c].rearrange("p (k c) -> p k c", k=k)

    def halves(pair, part=slice(0, P)):
        return [bank[2 * pair + h][part, 0:HALF] for h in range(2)]

    w_in = io["w_in"][0]
    ID5 = cst[0:5, K_SEL:K_SEL + 2 * P]
    RQ, RKV, R2, R3 = 8, 16, 40, 56
    kcol = [0, 128, 256, 384, 640, 512]
    stream = [0, 0, 0, 0, 1]
    spans = [(0, N_SAMPLE, 0), (N_SAMPLE, T, 1)]
    N_ADA1 = 8
    N_LAT, N_ADA2, N_UQ, N_UKV, N_ATT, N_CONV, N_G, N_M, N_MIX = 8, 10, 14, 15, 16, 24, 40, 48, 56
    units = [(h, i) for h in range(NH) for i in range(NT)]

    def nth(j0, d):
        return j0 + (d + 1)

    def nth_dma(j0, d, each=16):
        return j0 * (each // 2) + (each // 2 * (d - d % 2) + each)

    A, B, C = range(3)

    def wait_alone(eng, sem_, value):
        eng.wait_ge(sem_, value)
        eng.sem_inc(sp_turns if eng is nc.sync else pool_turns)

    def extra_of(eng):
        eng.wait_ge(s_extra, 1)
        return eng.value_load(extra_i[0:1, 0:1], min_val=0, max_val=X_MAX)

    def sp_moe(sp):
        def expert(ap, e, rows):
            return ap[0][bass.ds(e, 1), rows, :].rearrange("a (k p) c -> p (a k) c", p=P)

        def expert_of(j0, d):
            if isinstance(j0, int):
                return d
            return sp.value_load(expert_i[0:1, bass.ds(j0 + d, 1)], min_val=0, max_val=NE - 1)

        def load_up(kind, j0, d):
            if not (isinstance(j0, int) and d < 2):
                wait_alone(sp, w_done[1][kind], nth(j0, d - 2))
            e = expert_of(j0, d)
            t = v3(wr[kind][d % 2], 4, 2 * DE)
            rows = slice(kind * 512, (kind + 1) * 512)
            sp.dma_start(t[:, :, 0:DE], expert(io["w_up"], e, rows)).then_inc(wr_in[kind][d % 2], 16)
            sp.dma_start(t[:, :, DE:], expert(io["w_gate"], e, rows)).then_inc(wr_in[kind][d % 2], 16)

        def load_down(j0, d):
            if not (isinstance(j0, int) and d < 2):
                wait_alone(sp, w_done[1][C], nth(j0, d - 2))
            e = expert_of(j0, d)
            sp.dma_start(v3(wr[C][d % 2], 2, D), expert(io["w_down"], e, slice(0, DE))).then_inc(wr_in[C][d % 2], 16)

        load_up(A, 0, 0)
        load_up(B, 0, 0)
        load_up(A, 0, 1)
        sp.wait_ge(piece_used, N_MIX + 4)
        sp.dma_start(norm2_b[:, :], io["norm2"].partition_broadcast(P)).then_inc(s_n2, 16)
        sp.dma_start(wrt[:, :, 0:NG], io["w_grp"][0].rearrange("(k p) c -> p k c", p=P)).then_inc(s_wr, 16)
        sp.dma_start(wrt[:, :, NG:], io["w_exp"][0].rearrange("(k p) c -> p k c", p=P)).then_inc(s_wr, 16)
        load_up(B, 0, 1)
        sp.wait_ge(s_bcp, 16)
        load_down(0, 0)
        load_up(A, 0, 2)
        X = extra_of(sp)
        with sp.Fori(2, X + NE, 2) as j0:
            for d in range(2):
                load_up(B, j0, d)
                load_down(j0, d - 1)
                load_up(A, j0, d + 1)
        load_down(X, NE - 1)
        wait_alone(sp, w_done[1][B], X + NE)
        wait_alone(sp, w_done[1][C], X + NE)
        wait_alone(sp, w_done[1][A], X + (NE + 1))
        sp.dma_start(fn_b[:, :], io["final_norm"].partition_broadcast(P)).then_inc(s_fn, 16)
        for p in range(2):
            sp.wait_ge(sct[p], X * 8 + NE * 8)
        for i in range(NT):
            if i >= 2:
                sp.wait_ge(s_x2, i - 1)
            sp.dma_start(ya[i % 2][:, :, :].rearrange("p a c -> p (a c)"),
                         YD[2 * i * P:2 * (i + 1) * P, :].rearrange("(p a) c -> p (a c)", a=2)
                         ).then_inc(ya_in[i % 2], 16)
            if i >= 1:
                store(sp, i - 1)
        store(sp, NT - 1)
        sp.wait_ge(y_out[0], 16 * 3)
        sp.wait_ge(y_out[1], 16 * 2)
        sp.wait_ge(s_latw, 32)

    def store(sp, i):
        sp.wait_ge(s_yt, i + 1)
        dst = io["y_sample"][0, i * P:(i + 1) * P, :] if i < NTS else io["y_prompt"][0]
        sp.dma_start(dst, yt[i % 2][:, :]).then_inc(y_out[i % 2], 16)

    def pool_moe(pool):
        pool.wait_ge(s_fill, 1)
        pool.dma_start(LISTD.rearrange("(p a) c -> p (a c)", p=P), fill[:, :]).then_inc(s_fillw, 16)
        for i in range(NT):
            pool.wait_ge(s_h2, i + 1)
            pool.dma_start(H2D[i * P:(i + 1) * P, :], h2s[i % 2][:, :]).then_inc(h2_w[i % 2], 16)
        pool.wait_ge(s_fillw, 16)
        pool.wait_ge(s_rec, 1)
        for i in range(NT):
            for c in range(2):
                pool.indirect_dma_start(
                    out=LISTD, out_offset=bass.IndirectOffsetOnAxis(ap=rec_at[:, i, c:c + 1], axis=0),
                    in_=rec[:, i, c, :], in_offset=None, bounds_check=N_LIST - 1,
                    oob_is_err=False).then_inc(s_scat, 16)
        X = extra_of(pool)
        pool.wait_ge(s_scat, 16 * 2 * NT)
        for i in range(2):
            pool.wait_ge(h2_w[i], 16 * (3 - i))

        def list_load(t, s, j0, d):
            pool.dma_start(t[d % 2][:, :], LISTD[bass.ds(j0 * P + d * P, P), :]).then_inc(s[d % 2], 16)

        def gather(j0, d):
            p = d % 2
            wait_alone(pool, lg_in[p], nth_dma(j0, d))
            pool.indirect_dma_start(
                out=xg[p][:, :], out_offset=None, in_=H2D,
                in_offset=bass.IndirectOffsetOnAxis(ap=lst_g[p][:, 0:1].bitcast(U32), axis=0),
                bounds_check=T - 1, oob_is_err=False).then_inc(gat[p], 16)

        def lo_down(j0, d):
            pool.wait_ge(w_done[0][C], nth(j0, d))
            pool.tensor_sub(wl[C][:, :], wr[C][d % 2][:, :], wh[C][:, :].bitcast(F32)).then_inc(w_done[1][C], 1)

        def scatter(j0, d):
            p = d % 2
            pool.wait_ge(s_ya, nth(j0, d))
            wait_alone(pool, s_yd, nth(j0, d))
            pool.indirect_dma_start(
                out=YD, out_offset=bass.IndirectOffsetOnAxis(ap=lst_s[p][:, 1:2].bitcast(U32), axis=0),
                in_=yo[p][:, :], in_offset=None, bounds_check=2 * T - 1,
                oob_is_err=False).then_inc(sct[p], 16)

        def step(j0, d):
            first = isinstance(j0, int)
            if not (first and d < 1):
                pool.wait_ge(s_tr, nth(j0, d - 1))
            gather(j0, d + 1)
            pool.wait_ge(gat[d % 2], nth_dma(j0, d))
            list_load(lst_g, lg_in, j0, d + 2)
            if not (first and d < 1):
                if not (first and d < 3):
                    pool.wait_ge(sct[(d - 1) % 2], nth_dma(j0, d - 3))
                list_load(lst_s, ls_in, j0, d - 1)
                lo_down(j0, d - 1)
            if not (first and d < 2):
                scatter(j0, d - 2)

        list_load(lst_g, lg_in, 0, 0)
        list_load(lst_g, lg_in, 0, 1)
        pool.wait_ge(s_xg0, 2)
        gather(0, 0)
        for d in range(4):
            step(0, d)
        with pool.Fori(4, X + NE, 2) as j0:
            step(j0, 0)
            step(j0, 1)
        pool.wait_ge(sct[1], nth_dma(X, NE - 3))
        list_load(lst_s, ls_in, X, NE - 1)
        lo_down(X, NE - 1)
        scatter(X, NE - 2)
        scatter(X, NE - 1)
        pool.wait_ge(gat[0], X * 8 + (NE * 8 + 16))
        for p in range(2):
            pool.wait_ge(lg_in[p], X * 8 + (NE * 8 + 16))
            pool.wait_ge(sct[p], X * 8 + NE * 8)

    def pe_moe(pe):
        def prod(out, st, mv, first, last):
            pe.matmul(out, st[0], mv[0], start=first, stop=False)
            pe.matmul(out, st[0], mv[1], start=False, stop=False)
            return pe.matmul(out, st[1], mv[0], start=False, stop=last)

        for i in range(NT):
            pe.wait_ge(s_h2, i + 1)
            if i >= 2:
                pe.wait_ge(s_h2Te, i - 1)
            for k in range(KD):
                x = pe.transpose(bank[2 * (i % 2) + k // 4][:, (k % 4) * P:(k % 4 + 1) * P],
                                 h2s[i % 2][:, k * P:(k + 1) * P], ident)
            x.then_inc(s_h2T, 1)
        pe.wait_ge(s_wr, 32)
        pe.wait_ge(s_h2Te, NT)
        pe.wait_ge(s_bce, 16)
        for c in range(2):
            for k in range(KD):
                x = pe.matmul(bank[4 + c][0:NG + NE, 0:HALF], wrt[:, k, :], h2T[:, k, c * HALF:(c + 1) * HALF],
                              start=(k == 0), stop=(k == KD - 1))
        x.then_inc(s_lg, 1)
        pe.wait_ge(s_lge, 1)
        for i in range(NT):
            x = pe.transpose(bank[6][:, i * 36:i * 36 + 36], lg36[:, i * P:(i + 1) * P], ident[0:36, 0:36])
        x.then_inc(s_lgT, 1)
        pe.wait_ge(s_mask, 1)
        pe.wait_ge(s_tri, 3)
        for i in range(NT):
            for j in range(i):
                pe.matmul(bank[7][:, i * NE:(i + 1) * NE], one_b[:, :], mask[:, j, :], start=(j == 0), stop=False)
            pe.matmul(bank[7][:, i * NE:(i + 1) * NE], tri_b[:, :], mask[:, i, :], start=(i == 0), stop=True)
        for j in range(NT):
            x = pe.matmul(bank[7][:, NT * NE:(NT + 1) * NE], one_b[:, :], mask[:, j, :], start=(j == 0),
                          stop=(j == NT - 1))
        x.then_inc(s_pos, 1)

        def turn(j0, d):
            first = isinstance(j0, int)
            pe.wait_ge(gat[d % 2], nth_dma(j0, d))
            if not (first and d < 1):
                pe.wait_ge(s_xgl, nth(j0, d - 1))
            for k in range(KD):
                x = pe.transpose(bank[k // 4][:, (k % 4) * P:(k % 4 + 1) * P],
                                 xg[d % 2][:, k * P:(k + 1) * P], ident)
            x.then_inc(s_tr, 1)

        def up(kind, j0, d):
            first = isinstance(j0, int)
            pe.wait_ge(w_done[1][kind], nth(j0, d))
            if kind == A:
                pe.wait_ge(s_xgl, nth(j0, d))
                if not (first and d < 2):
                    pe.wait_ge(s_act, nth(j0, d - 2))
            wv = [v3(t[kind], 4, 2 * DE) for t in (wh, wl)]
            for k in range(4):
                x = prod(bank[2 + d % 2][:, :], [t[:, 4 * kind + k, :] for t in xgT[d % 2]],
                         [t[:, k, :] for t in wv], kind == A and k == 0, kind == B and k == 3)
            x.then_inc(w_done[2][kind], 1)

        def act_turn(j0, d):
            pe.wait_ge(s_act, nth(j0, d))
            if not (isinstance(j0, int) and d < 1):
                pe.wait_ge(s_aT, nth(j0, d - 1))
            for f in range(2):
                x = pe.transpose(bank[4][:, f * P:(f + 1) * P], act_v[d % 2][:, f * P:(f + 1) * P], ident)
            x.then_inc(s_at, 1)

        def down(j0, d):
            pe.wait_ge(w_done[1][C], nth(j0, d))
            pe.wait_ge(s_aT, nth(j0, d))
            if not (isinstance(j0, int) and d < 1):
                pe.wait_ge(s_ya, nth(j0, d - 1))
                pe.wait_ge(s_yd, nth(j0, d - 1))
            wv = [v3(t[C], 2, D) for t in (wh, wl)]
            for c in range(2):
                for f in range(2):
                    x = prod(bank[5 + c][:, :], [t[:, f, :] for t in actT],
                             [t[:, f, c * 512:(c + 1) * 512] for t in wv], f == 0, f == 1)
            x.then_inc(w_done[2][C], 1)

        def step(j0, d):
            first = isinstance(j0, int)
            turn(j0, d)
            if not (first and d < 2):
                down(j0, d - 2)
            up(A, j0, d)
            if not (first and d < 1):
                act_turn(j0, d - 1)
            up(B, j0, d)

        X = extra_of(pe)
        step(0, 0)
        step(0, 1)
        with pe.Fori(2, X + NE, 2) as j0:
            step(j0, 0)
            step(j0, 1)
        down(X, NE - 2)
        act_turn(X, NE - 1)
        down(X, NE - 1)

    def act_moe(act, link):
        act.wait_ge(piece_used, N_MIX + 4)
        for j in range(4, 16):
            act.wait_ge(s_bcp, j + 1)
            t = (None, shift2, gain2, gate2)[j // 4]
            c = (j // 2) % 2
            act.copy(t[:, j % 2, c * 512:(c + 1) * 512], bank[4 + j % 4][:, :]).then_inc(s_bce, 1)
        for i in range(NT):
            act.wait_ge(s_mixe, NT + i + 1)
            if i >= 2:
                act.wait_ge(s_h2T, i - 1)
                act.wait_ge(h2_w[i % 2], 16 * (i // 2))
            link(act.activation(h2s[i % 2][:, :], x1[:, i, :], ACT.Square, accum_out=stat[:, R2 + i:R2 + i + 1]))
            link(act.mul(stat[:, 80 + i:81 + i], stat[:, R2 + i:R2 + i + 1], 1.0 / D))
            act.activation(stat[:, R2 + 8 + i:R2 + 9 + i], stat[:, 80 + i:81 + i], ACT.Sqrt,
                           bias=stat[:, 95:96]).then_inc(s_rms2, 1)
            if i >= 1:
                h2T_out(act, i - 1)
        h2T_out(act, NT - 1)
        act.wait_ge(s_lg, 1)
        for c in range(2):
            x = act.copy(lg36[:, c * HALF:(c + 1) * HALF], bank[4 + c][0:NG + NE, 0:HALF])
        x.then_inc(s_lge, 1)
        act.wait_ge(s_gx_in, 1)
        act.activation(r_ge[:, :, :], r_gs[:, :, :], ACT.Exp).then_inc(s_gx, 1)
        act.wait_ge(s_dx_in, 1)
        act.activation(r5[4][:, :], r5[3][:, :], ACT.Exp).then_inc(s_dx, 1)

        def hi_of(kind, j0, d):
            act.wait_ge(wr_in[kind][d % 2], nth_dma(j0, d, 32 if kind < C else 16))
            if not (isinstance(j0, int) and d < 1):
                act.wait_ge(w_done[2][kind], nth(j0, d - 1))
            act.copy(wh[kind][:, :], wr[kind][d % 2][:, :]).then_inc(w_done[0][kind], 1)

        def silu(j0, d):
            act.wait_ge(w_done[2][B], nth(j0, d))
            if not (isinstance(j0, int) and d < 2):
                act.wait_ge(s_act, nth(j0, d - 2))
            act.activation(sa[d % 2][:, :], bank[2 + d % 2][:, DE:2 * DE], ACT.Silu).then_inc(s_si, 1)

        def xg_hi(j0, d):
            act.wait_ge(s_tr, nth(j0, d))
            for b in range(2):
                x = act.copy(xgT[d % 2][0][:, 4 * b:4 * b + 4, :], v3(bank[b], 4, P))
            x.then_inc(s_xgh, 1)

        def y_half(j0, d):
            act.wait_ge(w_done[2][C], nth(j0, d))
            act.wait_ge(ls_in[d % 2], nth_dma(j0, d))
            if not (isinstance(j0, int) and d < 2):
                act.wait_ge(sct[d % 2], nth_dma(j0, d - 2))
            act.activation(yo[d % 2][:, 0:512], bank[5][:, :], ACT.Copy,
                           scale=lst_s[d % 2][:, 2:3]).then_inc(s_ya, 1)

        def step(j0, d):
            first = isinstance(j0, int)
            if not (first and d < 1):
                silu(j0, d - 1)
            xg_hi(j0, d)
            hi_of(B, j0, d)
            if not (first and d < 2):
                y_half(j0, d - 2)
            if not (first and d < 1):
                hi_of(C, j0, d - 1)
            hi_of(A, j0, d + 1)

        X = extra_of(act)
        hi_of(A, 0, 0)
        step(0, 0)
        step(0, 1)
        with act.Fori(2, X + NE, 2) as j0:
            step(j0, 0)
            step(j0, 1)
        silu(X, NE - 1)
        y_half(X, NE - 2)
        hi_of(C, X, NE - 1)
        y_half(X, NE - 1)
        for i in range(NT):
            act.wait_ge(s_x2, i + 1)
            if i >= 2:
                act.wait_ge(y_out[i % 2], 16 * (i // 2))
            link(act.activation(yt[i % 2][:, :], x1[:, i, :], ACT.Square, accum_out=stat[:, R3 + i:R3 + i + 1]))
            link(act.mul(stat[:, 80 + i:81 + i], stat[:, R3 + i:R3 + i + 1], 1.0 / D))
            act.activation(stat[:, R3 + 8 + i:R3 + 9 + i], stat[:, 80 + i:81 + i], ACT.Sqrt,
                           bias=stat[:, 95:96]).then_inc(s_rms3, 1)

    def h2T_out(act, i):
        act.wait_ge(s_h2T, i + 1)
        for b in range(2):
            x = act.copy(h2T[:, 4 * b:4 * b + 4, i * P:(i + 1) * P], v3(bank[2 * (i % 2) + b], 4, P))
        x.then_inc(s_h2Te, 1)

    def dve_moe(dve, link):
        dve.wait_ge(s_bce, 16)
        dve.wait_ge(s_n2, 16)
        link(dve.scalar_tensor_tensor(out=gain2[:, :, :], in0=gain2[:, :, :], scalar=1.0,
                                      in1=norm2_b[:, :].unsqueeze(1).to_broadcast([P, 2, D]),
                                      op0=ALU.add, op1=ALU.mult))
        for i in range(NT):
            dve.wait_ge(s_rms2, i + 1)
            link(dve.reciprocal(stat[:, 64 + i:65 + i], stat[:, R2 + 8 + i:R2 + 9 + i]))
            link(dve.scalar_tensor_tensor(out=h2s[i % 2][:, :], in0=x1[:, i, :], scalar=stat[:, 64 + i:65 + i],
                                          in1=gain2[:, stream[i], :], op0=ALU.mult, op1=ALU.mult))
            dve.tensor_add(h2s[i % 2][:, :], h2s[i % 2][:, :], shift2[:, stream[i], :]).then_inc(s_h2, 1)

        dve.wait_ge(s_lgT, 1)
        link(dve.tensor_copy(lg[:, :, :], v3(bank[6], NT, NG + NE)))

        def wide(ap, n):
            return ap.unsqueeze(2).to_broadcast([P, NT, n])

        def pick(src, top, hot, n):
            link(dve.tensor_reduce(top, src, AXX, ALU.max))
            link(dve.tensor_tensor(hot, src, wide(top, n), ALU.is_equal))
            rev = cst[:, K_REV + NE - n:K_REV + NE].unsqueeze(1).to_broadcast([P, NT, n])
            link(dve.tensor_mul(r_t[:, :, 0:n], hot, rev))
            link(dve.tensor_reduce(r5[7][:, :], r_t[:, :, 0:n], AXX, ALU.max))
            link(dve.tensor_tensor(hot, r_t[:, :, 0:n], wide(r5[7][:, :], n), ALU.is_equal))

        gl, el = lg[:, :, 0:NG], lg[:, :, NG:]
        pick(gl, r5[0][:, :], r_gh[:, :, :], NG)
        dve.tensor_tensor(r_gs[:, :, :], gl, wide(r5[0][:, :], NG), ALU.subtract).then_inc(s_gx_in, 1)
        link(dve.tensor_scalar(r_gh[:, :, :], r_gh[:, :, :], BIG, -BIG, ALU.mult, ALU.add))
        link(dve.tensor_add(el.rearrange("p t (g e) -> p t g e", g=NG), el.rearrange("p t (g e) -> p t g e", g=NG),
                            r_gh[:, :, :].unsqueeze(3).to_broadcast([P, NT, NG, EPG])))
        pick(el, r5[1][:, :], hot[0][:, :, :], NE)
        link(dve.scalar_tensor_tensor(out=el, in0=hot[0][:, :, :], scalar=-4 * BIG, in1=el,
                                      op0=ALU.mult, op1=ALU.add))
        pick(el, r5[2][:, :], hot[1][:, :, :], NE)
        dve.tensor_sub(r5[3][:, :], r5[2][:, :], r5[1][:, :]).then_inc(s_dx_in, 1)
        dve.tensor_add(mask[:, :, :], hot[0][:, :, :], hot[1][:, :, :]).then_inc(s_mask, 1)
        dve.wait_ge(s_gx, 1)
        link(dve.tensor_reduce(r5[5][:, :], r_ge[:, :, :], AXX, ALU.add))
        dve.wait_ge(s_dx, 1)
        link(dve.tensor_scalar(r5[6][:, :], r5[4][:, :], 1.0, None, ALU.add))
        link(dve.tensor_mul(r5[6][:, :], r5[6][:, :], r5[5][:, :]))
        link(dve.memset(rec[:, :, :, :].rearrange("p t c f -> p (t c f)"), 0.0))
        link(dve.reciprocal(rec[:, :, 0, 2], r5[6][:, :]))
        link(dve.tensor_mul(rec[:, :, 1, 2], rec[:, :, 0, 2], r5[4][:, :]))
        for c in range(2):
            dve.tensor_copy(rec[:, :, c, 0].bitcast(U32), cst[:, K_TOK:K_TOK + NT].bitcast(U32))
            link(dve.tensor_copy(rec[:, :, c, 1].bitcast(U32), cst[:, K_DST + c:K_DST + 2 * NT:2].bitcast(U32)))
        dve.wait_ge(s_pos, 1)
        cnt = bank[7][:, NT * NE:(NT + 1) * NE]
        link(dve.tensor_scalar(r_x[0][:, :], cnt, float(P), None, ALU.is_gt))
        for r in range(2, NT):
            link(dve.scalar_tensor_tensor(out=r_x[0][:, :], in0=cnt, scalar=float(r * P), in1=r_x[0][:, :],
                                          op0=ALU.is_gt, op1=ALU.add))
        link(dve.tensor_copy(r_x[1][:, :], r_x[0][:, :]))
        a, b = 1, 2
        for sh in (1, 2, 4, 8, 16):
            dve.tensor_copy(r_x[b][:, 0:sh], r_x[a][:, 0:sh])
            link(dve.tensor_add(r_x[b][:, sh:], r_x[a][:, sh:], r_x[a][:, 0:NE - sh]))
            a, b = b, a
        incl = r_x[a]
        dve.tensor_sub(r_x[b][:, :], incl[:, :], r_x[0][:, :])
        link(dve.tensor_scalar(r1[:, 2:3], incl[:, NE - 1:NE], 0.0, 2.0, ALU.is_gt, ALU.mult))
        for r in range(2, X_MAX, 2):
            link(dve.tensor_scalar(r1[:, 1:2], incl[:, NE - 1:NE], float(r), 2.0, ALU.is_gt, ALU.mult))
            link(dve.tensor_add(r1[:, 2:3], r1[:, 2:3], r1[:, 1:2]))
        excl = r_x[b]
        iota = cst[:, K_IOTA:K_IOTA + NE]
        dve.tensor_copy(expert_i[:, 0:NE], iota)
        for q in range(X_MAX):
            dve.tensor_scalar(r_x[3][:, :], excl[:, :], float(q), None, ALU.is_le)
            link(dve.tensor_scalar(r_x[4][:, :], incl[:, :], float(q), None, ALU.is_gt))
            link(dve.tensor_mul(r_x[3][:, :], r_x[3][:, :], r_x[4][:, :]))
            link(dve.tensor_mul(r_x[3][:, :], r_x[3][:, :], iota))
            link(dve.tensor_reduce(r_e[:, q:q + 1], r_x[3][:, :], AXX, ALU.add))
        dve.memset(expert_i[:, NE + X_MAX:], 0)
        dve.tensor_copy(expert_i[:, NE:NE + X_MAX], r_e[:, :])
        link(dve.tensor_copy(extra_i[:, :], r1[:, 2:3]))
        dve.engine_nop().then_inc(s_extra, 1)
        pos = v3(bank[7], NT, NE)
        for c in range(2):
            def picked(dst, table):
                link(dve.tensor_mul(r_t[:, :, :], hot[c][:, :, :], table))
                link(dve.tensor_reduce(dst, r_t[:, :, :], AXX, ALU.add))

            picked(r5[5][:, :], pos)
            picked(r5[6][:, :], iota.unsqueeze(1).to_broadcast([P, NT, NE]))
            picked(r5[7][:, :], excl[:, :].unsqueeze(1).to_broadcast([P, NT, NE]))
            link(dve.scalar_tensor_tensor(out=r5[7][:, :], in0=r5[7][:, :], scalar=float(NE - 1), in1=r5[6][:, :],
                                          op0=ALU.add, op1=ALU.subtract))
            link(dve.scalar_tensor_tensor(out=r5[7][:, :], in0=r5[5][:, :], scalar=float(P), in1=r5[7][:, :],
                                          op0=ALU.is_ge, op1=ALU.mult))
            link(dve.tensor_add(r5[6][:, :], r5[6][:, :], r5[7][:, :]))
            link(dve.scalar_tensor_tensor(out=rec_at[:, :, c], in0=r5[6][:, :], scalar=float(P), in1=r5[5][:, :],
                                          op0=ALU.mult, op1=ALU.add))
        dve.engine_nop().then_inc(s_rec, 1)
        for i in range(2):
            dve.wait_ge(h2_w[i], 16 * (3 - i))
            dve.memset(xg[i][:, :], 0.0).then_inc(s_xg0, 1)

        def lo_of(kind, j0, d):
            dve.wait_ge(w_done[0][kind], nth(j0, d))
            dve.tensor_sub(wl[kind][:, :], wr[kind][d % 2][:, :], wh[kind][:, :].bitcast(F32)
                           ).then_inc(w_done[1][kind], 1)

        def gate_mul(j0, d):
            dve.wait_ge(s_si, nth(j0, d))
            if not (isinstance(j0, int) and d < 2):
                dve.wait_ge(s_at, nth(j0, d - 2))
            dve.tensor_mul(act_v[d % 2][:, :], bank[2 + d % 2][:, 0:DE], sa[d % 2][:, :]).then_inc(s_act, 1)

        def xg_lo(j0, d):
            dve.wait_ge(s_xgh, nth(j0, d))
            for b in range(2):
                x = dve.tensor_sub(xgT[d % 2][1][:, 4 * b:4 * b + 4, :], v3(bank[b], 4, P),
                                   xgT[d % 2][0][:, 4 * b:4 * b + 4, :].bitcast(F32))
            x.then_inc(s_xgl, 1)

        def act_out(j0, d):
            dve.wait_ge(s_at, nth(j0, d))
            if not (isinstance(j0, int) and d < 1):
                dve.wait_ge(w_done[2][C], nth(j0, d - 1))
            dve.tensor_copy(actT[0][:, :, :], v3(bank[4], 2, P)).then_inc(s_aTh, 1)
            dve.wait_ge(s_aTh, nth(j0, d))
            dve.tensor_sub(actT[1][:, :, :], v3(bank[4], 2, P), actT[0][:, :, :].bitcast(F32)).then_inc(s_aT, 1)

        def y_half(j0, d):
            dve.wait_ge(w_done[2][C], nth(j0, d))
            dve.wait_ge(ls_in[d % 2], nth_dma(j0, d))
            if not (isinstance(j0, int) and d < 2):
                dve.wait_ge(sct[d % 2], nth_dma(j0, d - 2))
            dve.tensor_scalar(yo[d % 2][:, 512:D], bank[6][:, :], lst_s[d % 2][:, 2:3], None,
                              ALU.mult).then_inc(s_yd, 1)

        def step(j0, d):
            first = isinstance(j0, int)
            if not (first and d < 1):
                gate_mul(j0, d - 1)
            xg_lo(j0, d)
            lo_of(B, j0, d)
            if not (first and d < 2):
                y_half(j0, d - 2)
            if not (first and d < 1):
                act_out(j0, d - 1)
            lo_of(A, j0, d + 1)

        X = extra_of(dve)
        lo_of(A, 0, 0)
        step(0, 0)
        step(0, 1)
        with dve.Fori(2, X + NE, 2) as j0:
            step(j0, 0)
            step(j0, 1)
        gate_mul(X, NE - 1)
        y_half(X, NE - 2)
        act_out(X, NE - 1)
        y_half(X, NE - 1)
        dve.wait_ge(s_fn, 16)
        for i in range(NT + 1):
            if i < NT:
                dve.wait_ge(ya_in[i % 2], 16 * (i // 2 + 1))
                t = ya[i % 2]
                link(dve.tensor_add(t[:, 0, :], t[:, 0, :], t[:, 1, :]))
                link(dve.tensor_mul(t[:, 0, :], t[:, 0, :], gate2[:, stream[i], :]))
                dve.tensor_add(x1[:, i, :], x1[:, i, :], t[:, 0, :]).then_inc(s_x2, 1)
            if i >= 1:
                n = i - 1
                dve.wait_ge(s_rms3, n + 1)
                link(dve.reciprocal(stat[:, 72 + n:73 + n], stat[:, R3 + 8 + n:R3 + 9 + n]))
                dve.scalar_tensor_tensor(out=yt[n % 2][:, :], in0=x1[:, n, :], scalar=stat[:, 72 + n:73 + n],
                                         in1=fn_b[:, :], op0=ALU.mult, op1=ALU.mult).then_inc(s_yt, 1)

    block = es.enter_context(nc.Block())

    @block.sync
    def _(sp):
        sp.dma_start(cst[:, :], io["consts"]).then_inc(s_cst, 16)
        sp.dma_start(vecs[0:8, :], io["c"][0].rearrange("(k p) -> k p", p=P)).then_inc(s_vec, 16)
        sp.dma_start(vecs[8:16, :], io["c_ctx"].rearrange("(k p) -> k p", p=P)).then_inc(s_vec, 16)
        sp.dma_start(vecs[16:24, :], io["norm1"][0].rearrange("(k p) -> k p", p=P)).then_inc(s_vec, 16)
        sp.dma_start(vecs[24:48, :], io["conv_w"][0].rearrange("w (k p) -> (w k) p", p=P)).then_inc(s_vec, 16)

        def x_rows(i):
            return io["x_sample"][0, i * P:(i + 1) * P, :] if i < NTS else io["x_prompt"][0]

        for i in range(NT):
            sp.dma_start(x_tok[:, i, :], x_rows(i)).then_inc(x_in[i], 16)

        def load(n, src, k, c, i=0, step=0):
            if n >= 4:
                wait_alone(sp, lo_done, i * step + (n - 3))
            sp.dma_start(v3(raw[n % 4], k, c), src).then_inc(raw_in[n % 4], 16)

        def kpc(ap):
            return ap.rearrange("(k p) c -> p k c", p=P)

        def ada(n, c):
            load(n, kpc(io["w_ada"][0][:, c * 256:(c + 1) * 256]), KD, 256)

        for c in range(N_ADA1):
            ada(c, c)
        for kh in range(2):
            load(N_LAT + kh, kpc(w_in[kh * 512:(kh + 1) * 512, C_LAT:C_LAT + LAT]), 4, LAT)
        sp.dma_start(qn_b[:, :], io["q_norm"].partition_broadcast(P)).then_inc(s_bc, 16)
        sp.dma_start(kvn_b[:, :], io["kv_norm"].partition_broadcast(P)).then_inc(s_bc, 16)
        for c in range(4):
            ada(N_ADA2 + c, N_ADA1 + c)
        sp.wait_ge(s_hlo, KD)
        sp.dma_start(lat[:, NT, QL:QL + KVL], io["cache_ckv"][0, 0]).then_inc(s_cache, 16)
        sp.dma_start(lat[:, NT, QL + KVL:LAT], io["cache_krope"][0, 0]).then_inc(s_cache, 16)
        load(N_UQ, kpc(io["w_uq"][0]), 2, NH * QK)
        sp.wait_ge(lo_done, N_UKV - 3)
        for e, s_in in enumerate((raw_in[N_UKV % 4], s_ukv_v)):
            sp.dma_start(v3(raw[N_UKV % 4][:, e * 512:], NH, 64),
                         io["w_ukv"][0].rearrange("p (h s c) -> s p h c", s=2, h=NH)[e]).then_inc(s_in, 16)
        for h in range(NH):
            ada(N_ATT + h, 12 + h)
        with sp.Fori(0, 4) as it:
            for q, c0 in enumerate((C_CG, C_U, C_BG)):
                load(N_CONV + q, kpc(w_in[:, bass.ds(it * 256 + c0, 256)]), KD, 256, it, 4)
            load(N_CONV + 3, kpc(io["w_ada"][0][:, bass.ds(it * 256 + 20 * 256, 256)]), KD, 256, it, 4)
        with sp.Fori(0, 2) as it:
            for mp in range(2):
                load(N_G + 2 * mp, kpc(w_in[:, bass.ds(it * 512 + (C_GC + mp * 256), 256)]), KD, 256, it, 4)
                load(N_G + 2 * mp + 1, kpc(io["w_conv_out"][0][:, bass.ds(it * 512 + mp * 256, 256)]),
                     KD, 256, it, 4)
        with sp.Fori(0, 2) as it:
            for mp in range(2):
                load(N_M + 2 * mp, kpc(w_in[:, bass.ds(it * 512 + (C_GM + mp * 256), 256)]), KD, 256, it, 4)
                load(N_M + 2 * mp + 1, kpc(io["w_o"][0][:, bass.ds(it * 512 + mp * 256, 256)]), 4, 256, it, 4)
        for c in range(2):
            for kh in range(2):
                load(N_MIX + 2 * c + kh,
                     kpc(io["w_mix_out"][0][kh * 512:(kh + 1) * 512, c * 512:(c + 1) * 512]), 4, 512)
        sp.wait_ge(s_mlo, KD)
        for i in range(NT):
            sp.dma_start(x1[:, i, :], x_rows(i)).then_inc(x_again[i], 16)

        sp_moe(sp)

    @block.gpsimd
    def _(pool):
        def mod_store(c):
            pool.wait_ge(stg_ready, c + 1)
            pool.dma_start(MODD[:, c * 256:(c + 1) * 256], stg[c % 2][:, :]).then_inc(mod_w[c % 2], 16)

        for c in range(N_ADA1):
            mod_store(c)
        for i in range(2):
            pool.wait_ge(mod_w[i], 16 * N_ADA1 // 2)
        pool.dma_start(mod1[0:4, :], MODD[:, 0:2 * D]).then_inc(s_mod1, 16)
        pool.dma_start(mod1[4:5, :], io["b_ada"][:, 0:2 * D]).then_inc(s_mod1, 16)
        pool.wait_ge(s_latn, NT)
        pool.dma_start(io["new_ckv"][0, 0], lat[:, NT - 1, QL:QL + KVL]).then_inc(s_latw, 16)
        pool.dma_start(io["new_krope"][0, 0], lat[:, NT - 1, QL + KVL:LAT]).then_inc(s_latw, 16)
        for c in range(N_ADA1, 20):
            mod_store(c)
        for i in range(2):
            pool.wait_ge(mod_w[i], 16 * 10)
        pool.wait_ge(stg_ready, 24)
        pool.dma_start(MODD[:, 20 * 256:24 * 256], stg_c[:, :]).then_inc(mod_c, 16)
        pool.wait_ge(mod_c, 16)
        pool.wait_ge(y_free, 16)
        pool.dma_start(modt[0:4, :], MODD[:, 2 * D:6 * D]).then_inc(s_modt, 16)
        pool.dma_start(modt[4:5, :], io["b_ada"][:, 2 * D:6 * D]).then_inc(s_modt, 16)
        pool_moe(pool)

    @block.tensor
    def _(pe):
        def prod(out, st, mv, first, last):
            pe.matmul(out, st[0], mv[0], start=first, stop=False)
            pe.matmul(out, st[0], mv[1], start=False, stop=False)
            return pe.matmul(out, st[1], mv[0], start=False, stop=last)

        def prod2(outs, st, mvs, first, last):
            for o, m in zip(outs, mvs):
                pe.matmul(o, st[0], m[0], start=first, stop=False)
            for o, m in zip(outs, mvs):
                pe.matmul(o, st[0], m[1], start=False, stop=False)
            for o, m in zip(outs, mvs):
                x = pe.matmul(o, st[1], m[0], start=False, stop=last)
            return x

        def ada(n, out, i=0, step=0):
            pe.wait_ge(lo_done, i * step + (n + 1))
            wh_, wl_ = v3(hi[n % 2], KD, 256), v3(lo[n % 2], KD, 256)
            def whole(k):
                return pe.matmul(out[0:4, :], cond4[:, k, :], wh_[:, k, :], start=(k == 0), stop=(k == KD - 1))

            x = whole(0)
            for k in range(KD):
                pe.matmul(out[0:2, :], cond4[:, k, 0:2], wl_[:, k, :], start=False, stop=False)
                if k:
                    x = whole(k)
            x.then_inc(piece_used, 1)

        pe.wait_ge(s_cst, 16)
        pe.wait_ge(s_vec, 64)
        pe.transpose(bank[7][:, 0:48], vecs[:, :], ident[0:48, 0:48]).then_inc(s_vT, 1)
        for i in range(NT):
            pe.wait_ge(s_xn, i + 1)
            if i >= 3:
                pe.wait_ge(s_xTe, i - 2)
            for k in range(KD):
                x = pe.transpose(bank[2 * (i % 3) + k // 4][:, (k % 4) * P:(k % 4 + 1) * P],
                                 x_tok[:, i, k * P:(k + 1) * P], ident)
            x.then_inc(s_xT, 1)
        pe.wait_ge(s_cond, 2)
        pe.wait_ge(c_vT, 1)
        for c in range(N_ADA1):
            if c >= 2:
                pe.wait_ge(stg_ready, c - 1)
            ada(c, bank[6 + c % 2][:, 0:256])
        pe.wait_ge(s_mod1, 32)
        pe.wait_ge(stg_ready, N_ADA1)
        for b in range(16):
            x = pe.matmul(bank[7][:, 2 * b:2 * b + 2], mod1[:, b * P:(b + 1) * P], ID5[:, 0:2 * P:P],
                          start=True, stop=True)
        x.then_inc(s_m1T, 1)

        pe.wait_ge(s_xTe, NT)
        for kh in range(2):
            n = N_LAT + kh
            pe.wait_ge(lo_done, n + 1)
            wv = [v3(t, 4, LAT) for t in (hi[n % 2], lo[n % 2])]
            for i in range(NT):
                for k in range(4):
                    kk = 4 * kh + k
                    if i == 0:
                        pe.wait_ge(s_hlo, kk + 1)
                    x = prod(bank[i][:, 0:LAT], [t[:, kk, i * P:(i + 1) * P] for t in hT],
                             [t[:, k, :] for t in wv], kk == 0, kk == KD - 1)
                if i == NT - 1:
                    x.then_inc(piece_used, 1)
                elif kh == 1:
                    x.then_inc(s_lat, 1)
        for c in range(4):
            pe.wait_ge(stg_ready, N_ADA1 + c - 1)
            ada(N_ADA2 + c, bank[6 + c % 2][:, 0:256])

        pe.wait_ge(stg_ready, N_ADA1 + 4)
        for i in range(NT + 1):
            b = bank[(5 + i) % 8]
            if i < NT:
                pe.wait_ge(s_latn, NT if i >= 3 else i + 1)
            else:
                pe.wait_ge(s_cache, 32)
            for k in range(2 if i < NT else 0):
                pe.transpose(b[:, k * P:(k + 1) * P], lat[:, i, k * P:(k + 1) * P], ident)
            pe.transpose(b[:, 256:384], lat[:, i, QL:QL + KVL], ident)
            pe.transpose(b[0:ROPE, 384:512], lat[:, i, QL + KVL:LAT], ident).then_inc(s_lT, 1)

        pe.wait_ge(s_lTe, NT + 1)
        pe.wait_ge(lo_done, N_UQ + 1)
        wq = [v3(t, 2, NH * QK) for t in (hi[N_UQ % 2], lo[N_UQ % 2])]

        def q_of(i):
            if i >= 2:
                pe.wait_ge(s_qr, i - 1)
            for c in range(2):
                for k in range(2):
                    x = prod(bank[2 * (i % 2) + c][:, 0:384], [t[:, k, i * P:(i + 1) * P] for t in cqT],
                             [t[:, k, c * 384:(c + 1) * 384] for t in wq], k == 0, k == 1)
            x.then_inc(s_q if i < NT - 1 else piece_used, 1)

        def q_turn(i):
            pe.wait_ge(s_qr, i + 1)
            if i >= 2:
                pe.wait_ge(s_tqe, i - 1)
            for h in range(NH):
                x = pe.transpose(bank[4 + 2 * (i % 2) + h // 4][0:QK, (h % 4) * P:(h % 4 + 1) * P],
                                 qtok[i % 2][:, h, :], ident)
            x.then_inc(s_tq, 1)

        q_of(0)
        for i in range(NT):
            if i + 1 < NT:
                q_of(i + 1)
            q_turn(i)

        pe.wait_ge(lo_done, N_UKV + 1)
        pe.wait_ge(s_qr, NT)
        wkv = (hi[N_UKV % 2], lo[N_UKV % 2])
        j = 0
        for hp in range(NH // 2):
            for c in range(2):
                if j >= 4:
                    pe.wait_ge(s_kve, j - 3)
                prod(bank[j % 4][:, 0:384], [t[:, hp * P:(hp + 1) * P] for t in wkv],
                     [t[:, c * 384:(c + 1) * 384] for t in ckvT], True, True).then_inc(s_kv, 1)
                j += 1
        for kt in range(NKT + 1):
            pe.wait_ge(s_kve, j - 3)
            prod(bank[j % 4][:, :], [t[:, kt * P:(kt + 1) * P] for t in ckvT],
                 [t[:, NH * NOPE:NH * P] for t in wkv], True, True).then_inc(s_kv if kt < NKT else piece_used, 1)
            j += 1

        def scores(n):
            h, i = units[n]
            if n >= 2:
                pe.wait_ge(s_ex, n - 1)
            qh = qT[:, h, i * P:(i + 1) * P]
            if i < NTS:
                for c in range(2):
                    x = pe.matmul(bank[2 * (n % 2) + c][:, 0:HALF], qh, kT[:, h, c * HALF:(c + 1) * HALF],
                                  start=True, stop=True)
            else:
                x = pe.matmul(bank[2 * (n % 2)][:, 0:P], qh, kT[:, h, KEYS:ALLK], start=True, stop=True)
            x.then_inc(s_sc, 1)

        def p_turn(n):
            h, i = units[n]
            pe.wait_ge(s_pn, n + 1)
            if n >= 1:
                pe.wait_ge(s_pe, n)
            for kt in range(NKT if i < NTS else 1):
                x = pe.transpose(bank[4 + kt // 4][:, (kt % 4) * P:(kt % 4 + 1) * P],
                                 prob[n % 2][:, kt * P:(kt + 1) * P], ident)
            x.then_inc(s_tp, 1)

        def pv_sample(h):
            pe.wait_ge(s_pe, h * NT + NTS)
            if h >= 1:
                pe.wait_ge(s_ol, 2 * h)
            for kt in range(NKT):
                x = pe.matmul(bank[6][0:VH, :], V[:, kt, h * VH:(h + 1) * VH], pT[:, kt, :],
                              start=(kt == 0), stop=(kt == NKT - 1))
            x.then_inc(s_pv, 1)

        def pv_prompt(h):
            pe.wait_ge(s_pe, h * NT + NT)
            pe.matmul(bank[7][0:VH, 0:P], V[:, NKT, h * VH:(h + 1) * VH], pT[:, 0, 0:P],
                      start=True, stop=True).then_inc(s_pv, 1)

        pe.wait_ge(s_kve, j)
        pe.wait_ge(s_tqe, NT)
        scores(0)
        scores(1)
        for n, (h, i) in enumerate(units):
            if n + 2 < len(units):
                scores(n + 2)
            if i == 2:
                pe.wait_ge(stg_ready, 12 + h)
                if h >= 1:
                    pe.wait_ge(s_ol, 2 * h)
                ada(N_ATT + h, bank[7][:, 256:512])
            p_turn(n)
            if i == NTS - 1:
                pv_sample(h)
            if i == NTS:
                pv_prompt(h)

        pe.wait_ge(s_ol, 2 * NH)
        with pe.Fori(0, 4) as it:
            q = 0
            for p in range(3):
                n = N_CONV + p
                pe.wait_ge(lo_done, it * 4 + (n + 1))
                wv = [v3(t, KD, 256) for t in (hi[n % 2], lo[n % 2])]
                for mm in range(2):
                    pe.wait_ge(blk_free, it * 6 + max(q - 3, 0))
                    if q == 2:
                        pe.wait_ge(stg_ready, it + 20)
                    for k in range(KD):
                        x = prod2(halves(q % 4), [t[:, k, mm * P:(mm + 1) * P] for t in wv],
                                  [[t[:, k, c * HALF:(c + 1) * HALF] for t in hT] for c in range(2)],
                                  k == 0, k == KD - 1)
                    x.then_inc(piece_used if mm else blk_done, 1)
                    q += 1
            pe.wait_ge(stg_ready, it + 20)
            pe.wait_ge(blk_free, it * 6 + 3)
            ada(N_CONV + 3, bank[4][:, 0:256], it, 4)

        pe.wait_ge(blk_free, 24)
        pe.wait_ge(stg_ready, 24)
        for n0, kd, mv, g in ((N_G, KD, cT, 0), (N_M, 4, oT, 1)):
            with pe.Fori(0, 2) as it:
                for mp in range(2):
                    for kind, (free, done, kk, rhs) in enumerate(((gate_free, gate_done, KD, hT),
                                                                  (y_free, y_done, kd, mv))):
                        n = n0 + 2 * mp + kind
                        pe.wait_ge(lo_done, it * 4 + (n + 1))
                        wv = [v3(t, kk, 256) for t in (hi[n % 2], lo[n % 2])]
                        for mm in range(2):
                            if g or mp:
                                pe.wait_ge(free, it * 4 + (8 * g + 2 * mp + mm - 1))
                            else:
                                pe.wait_ge(free, it * (3 + mm))
                            for k in range(kk):
                                x = prod2(halves(2 * kind + mm), [t[:, k, mm * P:(mm + 1) * P] for t in wv],
                                          [[t[:, k, c * HALF:(c + 1) * HALF] for t in rhs] for c in range(2)],
                                          k == 0, k == kk - 1)
                            x.then_inc(piece_used if mm else done, 1)

        pe.wait_ge(y_free, 16)
        pe.wait_ge(gate_free, 16)
        pe.wait_ge(s_modt, 32)

        def bcast(j, part, c):
            pe.matmul(bank[4 + j % 4][:, :], ID5[:, (j % 2) * P:(j % 2 + 1) * P],
                      modt[:, part * D + c * 512:part * D + (c + 1) * 512], start=True,
                      stop=True).then_inc(s_bcp, 1)

        for j in range(4):
            bcast(j, 0, j // 2)

        for c in range(2):
            for kh in range(2):
                n = N_MIX + 2 * c + kh
                pe.wait_ge(lo_done, n + 1)
                wv = [v3(t, 4, 512) for t in (hi[n % 2], lo[n % 2])]
                for i in range(NT):
                    j = 5 * c + i
                    if kh == 0 and j >= 8:
                        pe.wait_ge(s_mixe, j - 7)
                    if kh == 0 and c == 0 and i == 4:
                        pe.wait_ge(s_bce, 4)
                    for k in range(4):
                        kk = 4 * kh + k
                        if c == 0 and i == 0:
                            pe.wait_ge(s_mlo, kk + 1)
                        x = prod(bank[j % 8][:, :], [t[:, kk, i * P:(i + 1) * P] for t in hT],
                                 [t[:, k, :] for t in wv], kk == 0, kk == KD - 1)
                    if i == NT - 1:
                        x.then_inc(piece_used, 1)
                    elif kh == 1:
                        x.then_inc(s_mix, 1)
        for j in range(4, 16):
            if j == 4:
                pe.wait_ge(s_mixe, 10)
            if j >= 8:
                pe.wait_ge(s_bce, j - 3)
            bcast(j, j // 4, (j // 2) % 2)
        pe_moe(pe)

    @block.scalar
    def _(act):
        links = [0]

        def link(x):
            links[0] += 1
            x.then_inc(achain, 1)
            act.wait_ge(achain, links[0])

        def split_hi(n, size, i=0, step=0):
            act.wait_ge(raw_in[n % 4], i * (4 * step) + 16 * (n // 4 + 1))
            if n >= 2:
                act.wait_ge(piece_used, i * step + (n - 1))
            act.copy(hi[n % 2][:, 0:size], raw[n % 4][:, 0:size]).then_inc(hi_done, 1)

        act.wait_ge(c_vT, 1)
        act.activation(cond2[:, :, :].rearrange("p k s -> p s k"),
                       vT[:, 0:16].rearrange("p (s k) -> p s k", s=2), ACT.Silu).then_inc(s_cond2, 1)
        for i in range(NT):
            act.wait_ge(x_in[i], 16)
            link(act.activation(sq0[:, :], x_tok[:, i, :], ACT.Square, accum_out=stat[:, i:i + 1]))
        link(act.mul(stat[:, 80:85], stat[:, 0:NT], 1.0 / D))
        act.wait_ge(s_tri, 3)
        act.activation(stat[:, 0:NT], stat[:, 80:85], ACT.Sqrt, bias=stat[:, 95:96]).then_inc(s_rms0, 1)
        split_hi(0, PIECE)
        split_hi(1, PIECE)
        for i in range(NT):
            act.wait_ge(s_xT, i + 1)
            for b in range(2):
                x = act.copy(xnT[:, 4 * b:4 * b + 4, i * P:(i + 1) * P],
                             v3(bank[2 * (i % 3) + b], 4, P))
            x.then_inc(s_xTe, 1)
        for n in range(2, N_LAT):
            split_hi(n, PIECE)
        for kh in range(2):
            split_hi(N_LAT + kh, 4 * LAT)
        for k in range(KD):
            act.wait_ge(s_aff, k + 1)
            act.copy(hT[0][:, k, :], xnT[:, k, :]).then_inc(s_hhi, 1)
        split_hi(N_ADA2, PIECE)
        for i in range(NT):
            act.wait_ge(s_lat, i + 1) if i < NT - 1 else act.wait_ge(piece_used, N_LAT + 2)
            if i == 0:
                act.wait_ge(s_hlo, KD)
            link(act.activation(qtok[0][:, 0:2, :].rearrange("p a b -> p (a b)")[:, 0:128], bank[i][:, 256:384],
                                ACT.Square, accum_out=stat[:, RKV + i:RKV + i + 1]))
            link(act.activation(qtok[0][:, 0:3, :].rearrange("p a b -> p (a b)")[:, 0:256], bank[i][:, 0:256],
                                ACT.Square, accum_out=stat[:, RQ + i:RQ + i + 1]))
        link(act.mul(stat[:, 80:85], stat[:, RQ:RQ + NT], 1.0 / QL))
        link(act.mul(stat[:, 85:90], stat[:, RKV:RKV + NT], 1.0 / KVL))
        act.activation(stat[:, RQ:RQ + NT], stat[:, 80:85], ACT.Sqrt, bias=stat[:, 95:96])
        act.activation(stat[:, RKV:RKV + NT], stat[:, 85:90], ACT.Sqrt, bias=stat[:, 95:96]).then_inc(s_rmsl, 1)
        for c in range(1, 4):
            split_hi(N_ADA2 + c, PIECE)
        split_hi(N_UQ, 2 * NH * QK)
        act.wait_ge(s_ukv_v, 16)
        split_hi(N_UKV, NH * P)
        for i in range(NT + 1):
            b = bank[(5 + i) % 8]
            act.wait_ge(s_lT, i + 1)
            if i < NT:
                act.copy(cqT[0][:, :, i * P:(i + 1) * P], v3(b, 2, P))
            act.copy(ckvT[0][:, kcol[i]:kcol[i] + P], b[:, 256:384]).then_inc(s_lTh, 1)
        for i in range(NT):
            act.wait_ge(s_tq, i + 1)
            for b in range(2):
                x = act.copy(qT[:, 4 * b:4 * b + 4, i * P:(i + 1) * P], v3(bank[4 + 2 * (i % 2) + b], 4, P)[0:QK])
            x.then_inc(s_tqe, 1)
        j = 0
        for hp in range(NH // 2):
            for c in range(2):
                act.wait_ge(s_kv, j + 1)
                for e in range(2):
                    x = act.copy(kT[0:NOPE, 2 * hp + e, c * 384:(c + 1) * 384],
                                 bank[j % 4][e * 64:e * 64 + 64, 0:384])
                x.then_inc(s_kve, 1)
                j += 1
        for kt in range(NKT + 1):
            act.wait_ge(s_kv, j + 1) if kt < NKT else act.wait_ge(piece_used, N_UKV + 1)
            act.copy(V[:, kt, :], bank[j % 4][:, :]).then_inc(s_kve, 1)
            j += 1
        for n, (h, i) in enumerate(units):
            if i == 1:
                split_hi(N_ATT + h, PIECE)
            act.wait_ge(s_mx, n + 1)
            if n >= 2:
                act.wait_ge(s_tp, n - 1)
            b = n % 2
            st = 20 + 4 * b
            if i < NTS:
                for c in range(2):
                    x = act.activation(prob[b][:, c * HALF:(c + 1) * HALF], bank[2 * b + c][:, 0:HALF], ACT.Exp,
                                       bias=stat[:, st:st + 1], scale=SCALE,
                                       accum_out=stat[:, st + 1 + c:st + 2 + c])
            else:
                x = act.activation(prob[b][:, 0:P], bank[2 * b][:, 0:P], ACT.Exp, bias=stat[:, st:st + 1],
                                   scale=SCALE, accum_out=stat[:, st + 1:st + 2])
            x.then_inc(s_ex, 1)
            if i == NTS:
                r = (h % 2) * 64
                act.wait_ge(s_pv, 2 * h + 1)
                act.copy(oT[0][r:r + 64, h // 2, 0:N_SAMPLE], bank[6][0:VH, :]).then_inc(s_oh, 1)
                act.wait_ge(s_pv, 2 * h + 2)
                act.copy(oT[0][r:r + 64, h // 2, N_SAMPLE:T], bank[7][0:VH, 0:P]).then_inc(s_oh, 1)
        for n in range(2):
            split_hi(N_CONV + n, PIECE)
        with act.Fori(0, 4) as it:
            for q in range(4):
                split_hi(N_CONV + 2 + q, PIECE, it, 4)
        for n0, g in ((N_G, 0), (N_M, 1)):
            with act.Fori(0, 2) as it:
                for mp in range(2):
                    for mm in range(2):
                        jj = 8 * g + 2 * mp + mm
                        if mm:
                            act.wait_ge(piece_used, it * 4 + (n0 + 2 * mp + 1))
                        else:
                            act.wait_ge(gate_done, it * 2 + (4 * g + mp + 1))
                        if g or mp:
                            act.wait_ge(y_free, it * 4 + (jj - 1))
                        else:
                            act.wait_ge(y_free, it * (3 + mm))
                        for c, o in enumerate(halves(mm)):
                            x = act.activation(sg[mm][:, c * HALF:(c + 1) * HALF], o, ACT.Sigmoid)
                        x.then_inc(gate_free, 1)
                    split_hi(n0 + 2 * mp + 2, PIECE, it, 4)
                    split_hi(n0 + 2 * mp + 3, PIECE, it, 4)
        for k in range(KD):
            if k == 0:
                act.wait_ge(y_free, 16)
            act.copy(hT[0][:, k, :], merged[:, k, :]).then_inc(s_mhi, 1)
        for j in range(4):
            act.wait_ge(s_bcp, j + 1)
            act.copy(gate1[:, j % 2, (j // 2) * 512:(j // 2 + 1) * 512], bank[4 + j % 4][:, :]).then_inc(s_bce, 1)
        for k in range(2, 4):
            split_hi(N_MIX + k, PIECE)
        act_moe(act, link)

    @block.vector
    def _(dve):
        links = [0]
        base = [0, 0]

        def link(x):
            links[0] += 1
            x.then_inc(dchain, 1)
            dve.wait_ge(dchain, base[0] * base[1] + links[0] if base[1] else links[0])

        def split_lo(n, size, i=0, step=0):
            dve.wait_ge(hi_done, i * step + (n + 1))
            dve.tensor_sub(lo[n % 2][:, 0:size], raw[n % 4][:, 0:size],
                           hi[n % 2][:, 0:size].bitcast(F32)).then_inc(lo_done, 1)

        def ada_out(n, c, b):
            dve.wait_ge(piece_used, n + 1)
            if c >= 2:
                dve.wait_ge(mod_w[c % 2], 16 * (c // 2))
            dve.tensor_copy(stg[c % 2][:, :], b[0:4, :]).then_inc(stg_ready, 1)

        dve.memset(stat[:, 95:96], EPS).then_inc(s_tri, 1)
        dve.memset(fill[:, :].bitcast(U32), FAR).then_inc(s_fill, 1)
        dve.wait_ge(s_cst, 16)
        dve.tensor_copy(tri_b[:, :], cst[:, K_TRI:K_TRI + P]).then_inc(s_tri, 1)
        dve.tensor_copy(one_b[:, :], cst[:, K_ONE:K_ONE + P]).then_inc(s_tri, 1)
        dve.wait_ge(s_vT, 1)
        dve.tensor_copy(vT[:, :], bank[7][:, 0:48]).then_inc(c_vT, 1)
        dve.wait_ge(s_cond2, 1)
        dve.tensor_copy(cond4[:, :, 0:2], cond2[:, :, :]).then_inc(s_cond, 1)
        dve.wait_ge(s_cond, 1)
        dve.tensor_sub(cond4[:, :, 2:4], cond2[:, :, :], cond4[:, :, 0:2].bitcast(F32)).then_inc(s_cond, 1)
        dve.wait_ge(s_rms0, 1)
        link(dve.reciprocal(stat[:, 32:37], stat[:, 0:NT]))
        for i in range(NT):
            dve.tensor_scalar(x_tok[:, i, :], x_tok[:, i, :], stat[:, 32 + i:33 + i], None,
                              ALU.mult).then_inc(s_xn, 1)
        split_lo(0, PIECE)
        split_lo(1, PIECE)
        for c in range(N_ADA1):
            ada_out(c, c, bank[6 + c % 2][:, 0:256])
            split_lo(c + 2, PIECE if c + 2 < N_LAT else 4 * LAT)
        dve.wait_ge(s_m1T, 1)
        link(dve.tensor_copy(shsc[:, :, :], v3(bank[7], 16, 2)))
        link(dve.scalar_tensor_tensor(out=gain1[:, :, :], in0=shsc[:, 8:16, :], scalar=1.0,
                                      in1=vT[:, 16:24].unsqueeze(2).to_broadcast([P, KD, 2]),
                                      op0=ALU.add, op1=ALU.mult))
        dve.wait_ge(s_xTe, NT)

        def h_lo(k):
            dve.wait_ge(s_hhi, k + 1)
            dve.tensor_sub(hT[1][:, k, :], xnT[:, k, :], hT[0][:, k, :].bitcast(F32)).then_inc(s_hlo, 1)

        for k in range(KD):
            for a, z, s in spans:
                x = dve.tensor_scalar(xnT[:, k, a:z], xnT[:, k, a:z], gain1[:, k, s:s + 1], shsc[:, k, s:s + 1],
                                      ALU.mult, ALU.add)
            x.then_inc(s_aff, 1)
            if k:
                h_lo(k - 1)
        h_lo(KD - 1)
        split_lo(N_ADA2, PIECE)

        def rope(dst, src, i, nh):
            cos, sin = (cst[:, k + 16 * i:k + 16 * i + 16].rearrange("p (a f) -> p a f", a=2)
                        .unsqueeze(1).to_broadcast([P, nh, 2, 8]) for k in (K_COS, K_SIN))
            for r, (half, tab) in enumerate(((0, cos), (1, sin), (1, cos), (0, sin))):
                x = dve.tensor_tensor(rt[r][:, 0:nh], src[:, :, :, half, :], tab, ALU.mult)
            link(x)
            dve.tensor_sub(dst[:, :, :, 0, :], rt[0][:, 0:nh], rt[1][:, 0:nh])
            return dve.tensor_add(dst[:, :, :, 1, :], rt[2][:, 0:nh], rt[3][:, 0:nh])

        def halfview(ap, nh):
            return ap.rearrange("p h (a b f) -> p h a b f", a=2, b=2)

        dve.wait_ge(s_bc, 32)
        dve.wait_ge(s_rmsl, 1)
        dve.reciprocal(stat[:, 32:37], stat[:, RQ:RQ + NT])
        link(dve.reciprocal(stat[:, 37:42], stat[:, RKV:RKV + NT]))
        for i in range(NT):
            b = bank[i]
            dve.scalar_tensor_tensor(out=lat[:, i, 0:QL], in0=b[:, 0:QL], scalar=stat[:, 32 + i:33 + i],
                                     in1=qn_b[:, :], op0=ALU.mult, op1=ALU.mult)
            dve.scalar_tensor_tensor(out=lat[:, i, QL:QL + KVL], in0=b[:, QL:QL + KVL],
                                     scalar=stat[:, 37 + i:38 + i], in1=kvn_b[:, :], op0=ALU.mult, op1=ALU.mult)
            if i < NTS:
                x = rope(halfview(lat[:, i:i + 1, QL + KVL:LAT], 1),
                         halfview(b[:, QL + KVL:LAT].unsqueeze(1), 1), i, 1)
                link(x)
                dve.engine_nop().then_inc(s_latn, 1)
            else:
                dve.tensor_copy(lat[:, i, QL + KVL:LAT], b[:, QL + KVL:LAT]).then_inc(s_latn, 1)
        split_lo(N_ADA2 + 1, PIECE)
        for c in range(4):
            ada_out(N_ADA2 + c, N_ADA1 + c, bank[6 + c % 2][:, 0:256])
            if c < 2:
                split_lo(N_ADA2 + 2 + c, PIECE)
        split_lo(N_UQ, 2 * NH * QK)
        split_lo(N_UKV, NH * P)
        for i in range(NT + 1):
            b = bank[(5 + i) % 8]
            dve.wait_ge(s_lTh, i + 1)
            if i < NT:
                dve.tensor_sub(cqT[1][:, :, i * P:(i + 1) * P], v3(b, 2, P),
                               cqT[0][:, :, i * P:(i + 1) * P].bitcast(F32))
            dve.tensor_sub(ckvT[1][:, kcol[i]:kcol[i] + P], b[:, 256:384],
                           ckvT[0][:, kcol[i]:kcol[i] + P].bitcast(F32))
            dve.tensor_copy(kT[NOPE:QK, :, kcol[i]:kcol[i] + P],
                            b[0:ROPE, 384:512].unsqueeze(1).to_broadcast([ROPE, NH, P])).then_inc(s_lTe, 1)
        for i in range(NT):
            dve.wait_ge(s_q, i + 1) if i < NT - 1 else dve.wait_ge(piece_used, N_UQ + 1)
            if i >= 2:
                dve.wait_ge(s_tq, i - 1)
            for c in range(2):
                src = v3(bank[2 * (i % 2) + c], 4, QK)
                dst = qtok[i % 2][:, 4 * c:4 * c + 4, :]
                if i < NTS:
                    dve.tensor_copy(dst[:, :, 0:NOPE], src[:, :, 0:NOPE])
                    x = rope(halfview(dst[:, :, NOPE:QK], 4), halfview(src[:, :, NOPE:QK], 4), i, 4)
                    link(x)
                else:
                    x = link(dve.tensor_copy(dst, src))
            dve.engine_nop().then_inc(s_qr, 1)
        def top(n):
            h, i = units[n]
            b, st = n % 2, 20 + 4 * (n % 2)
            if i == 1:
                split_lo(N_ATT + h, PIECE)
            dve.wait_ge(s_sc, n + 1)
            if i < NTS:
                for c in range(2):
                    x = dve.tensor_reduce(stat[:, 42 + 2 * b + c:43 + 2 * b + c], bank[2 * b + c][:, 0:HALF],
                                          AXX, ALU.max)
                link(x)
                link(dve.tensor_reduce(stat[:, 46 + b:47 + b], stat[:, 42 + 2 * b:44 + 2 * b], AXX, ALU.max))
            else:
                link(dve.tensor_reduce(stat[:, 46 + b:47 + b], bank[2 * b][:, 0:P], AXX, ALU.max))
            dve.tensor_scalar(stat[:, st:st + 1], stat[:, 46 + b:47 + b], -SCALE, None,
                              ALU.mult).then_inc(s_mx, 1)

        top(0)
        for n, (h, i) in enumerate(units):
            b, st = n % 2, 20 + 4 * (n % 2)
            if n + 1 < len(units):
                top(n + 1)
            dve.wait_ge(s_ex, n + 1)
            w = KEYS if i < NTS else P
            if i < NTS:
                link(dve.tensor_add(stat[:, st + 3:st + 4], stat[:, st + 1:st + 2], stat[:, st + 2:st + 3]))
                link(dve.reciprocal(stat[:, 48 + b:49 + b], stat[:, st + 3:st + 4]))
            else:
                link(dve.reciprocal(stat[:, 48 + b:49 + b], stat[:, st + 1:st + 2]))
            dve.tensor_scalar(prob[b][:, 0:w], prob[b][:, 0:w], stat[:, 48 + b:49 + b], None,
                              ALU.mult).then_inc(s_pn, 1)
            dve.wait_ge(s_tp, n + 1)
            if i == 0 and h >= 1:
                dve.wait_ge(s_pv, 2 * h)
            if i < NTS:
                dve.tensor_copy(pT[:, 0:4, i * P:(i + 1) * P], v3(bank[4], 4, P))
                dve.tensor_copy(pT[:, 4, i * P:(i + 1) * P], bank[5][:, 0:P]).then_inc(s_pe, 1)
            else:
                dve.wait_ge(s_pv, 2 * h + 1)
                dve.tensor_copy(pT[:, 0, 0:P], bank[4][:, 0:P]).then_inc(s_pe, 1)
            if i == 2:
                ada_out(N_ATT + h, 12 + h, bank[7][:, 256:512])
            if i == NTS:
                r = (h % 2) * 64
                for e, (b_, a, z) in enumerate(((6, 0, N_SAMPLE), (7, N_SAMPLE, T))):
                    dve.wait_ge(s_oh, 2 * h + e + 1)
                    dve.tensor_sub(oT[1][r:r + 64, h // 2, a:z], bank[b_][0:VH, 0:z - a],
                                   oT[0][r:r + 64, h // 2, a:z].bitcast(F32)).then_inc(s_ol, 1)
        for t in u:
            for a in (0, 513, 643):
                link(dve.memset(t[:, a:a + (2 if a == 513 else 1)], 0.0))
        LINKS_CONV = 10
        for n in range(2):
            split_lo(N_CONV + n, PIECE)

        def freed(x, n):
            x.then_inc(blk_free, 1)
            dve.wait_ge(blk_free, it * 6 + n)

        def blk_wait(p, mm):
            if mm:
                dve.wait_ge(piece_used, it * 4 + (N_CONV + p + 1))
            else:
                dve.wait_ge(blk_done, it * 3 + (p + 1))

        with dve.Fori(0, 4) as it:
            base[:] = it, LINKS_CONV
            l0 = links[0]
            for mm in range(2):
                blk_wait(0, mm)
                for c, o in enumerate(halves(mm)):
                    x = dve.tensor_copy(cg_s[mm][:, c * HALF:(c + 1) * HALF], o)
                freed(x, mm + 1)
            split_lo(N_CONV + 2, PIECE, it, 4)
            for mm in range(2):
                blk_wait(1, mm)
                o = halves(2 + mm)
                dve.tensor_mul(u[mm][:, 1:1 + HALF], o[0], cg_s[mm][:, 0:HALF])
                dve.tensor_mul(u[mm][:, 1 + HALF:1 + N_SAMPLE], o[1][:, 0:N_SAMPLE - HALF],
                               cg_s[mm][:, HALF:N_SAMPLE])
                freed(dve.tensor_mul(u[mm][:, 3 + N_SAMPLE:3 + T], o[1][:, N_SAMPLE - HALF:HALF],
                                     cg_s[mm][:, N_SAMPLE:T]), mm + 3)
                W = T + 2
                cw = [vT[:, bass.ds(it * 2 + (24 + 8 * tap + mm), 1)] for tap in range(3)]
                link(dve.tensor_scalar(cv[mm][:, :], u[mm][:, 0:W], cw[0], None, ALU.mult))
                for tap in (1, 2):
                    link(dve.scalar_tensor_tensor(out=cv[mm][:, :], in0=u[mm][:, tap:tap + W], scalar=cw[tap],
                                                  in1=cv[mm][:, :], op0=ALU.mult, op1=ALU.add))
            split_lo(N_CONV + 3, PIECE, it, 4)
            for mm in range(2):
                blk_wait(2, mm)
                o = halves(mm)
                prod_ = cg_s[mm]
                dve.tensor_mul(prod_[:, 0:HALF], o[0], cv[mm][:, 0:HALF])
                dve.tensor_mul(prod_[:, HALF:N_SAMPLE], o[1][:, 0:N_SAMPLE - HALF], cv[mm][:, HALF:N_SAMPLE])
                link(dve.tensor_mul(prod_[:, N_SAMPLE:T], o[1][:, N_SAMPLE - HALF:HALF],
                                    cv[mm][:, N_SAMPLE + 2:T + 2]))
                c_hi, c_lo = (t[:, bass.ds(it * 2 + mm, 1), :].rearrange("p a t -> p (a t)") for t in cT)
                link(dve.tensor_copy(c_hi, prod_[:, :]))
                dve.tensor_sub(c_lo, prod_[:, :], c_hi.bitcast(F32)).then_inc(blk_free, 1)
            split_lo(N_CONV + 4, PIECE, it, 4)
            dve.wait_ge(piece_used, it * 4 + (N_CONV + 4))
            dve.tensor_copy(stg_c[:, bass.ds(it * 256, 256)], bank[4][0:4, 0:256]).then_inc(stg_ready, 1)
            split_lo(N_CONV + 5, PIECE, it, 4)
            assert links[0] - l0 == LINKS_CONV, links[0] - l0
        base[:] = 0, 0
        links[0] = l0 + 4 * LINKS_CONV
        dve.wait_ge(mod_c, 16)
        LINKS_GATE = 8
        for n0, g in ((N_G, 0), (N_M, 1)):
            with dve.Fori(0, 2) as it:
                base[:] = it, LINKS_GATE * g
                l0 = links[0]
                for mp in range(2):
                    split_lo(n0 + 2 * mp + 2, PIECE, it, 4)
                    for mm in range(2):
                        jj = 8 * g + 2 * mp + mm
                        if mm:
                            dve.wait_ge(piece_used, it * 4 + (n0 + 2 * mp + 2))
                        else:
                            dve.wait_ge(y_done, it * 2 + (4 * g + mp + 1))
                        dve.wait_ge(gate_free, it * 4 + (jj + 1))
                        m = merged[:, bass.ds(it * 4 + (2 * mp + mm), 1), :].rearrange("p a t -> p (a t)")
                        for c, o in enumerate(halves(2 + mm)):
                            cs = slice(c * HALF, (c + 1) * HALF)
                            if g:
                                x = dve.tensor_mul(sg[mm][:, cs], o, sg[mm][:, cs])
                                link(x)
                                x = dve.tensor_add(m[:, cs], m[:, cs], sg[mm][:, cs])
                            else:
                                x = dve.tensor_mul(m[:, cs], o, sg[mm][:, cs])
                        x.then_inc(y_free, 1)
                    split_lo(n0 + 2 * mp + 3, PIECE, it, 4)
                if g:
                    assert links[0] - l0 == LINKS_GATE, links[0] - l0
        base[:] = 0, 0
        links[0] = l0 + 2 * LINKS_GATE
        for k in range(KD):
            dve.wait_ge(s_mhi, k + 1)
            dve.tensor_sub(hT[1][:, k, :], merged[:, k, :], hT[0][:, k, :].bitcast(F32)).then_inc(s_mlo, 1)
        split_lo(N_MIX + 2, PIECE)
        for c in range(2):
            for i in range(NT):
                dve.wait_ge(s_mix, 4 * c + i + 1) if i < NT - 1 else dve.wait_ge(piece_used, N_MIX + 2 * c + 2)
                if c == 0:
                    dve.wait_ge(x_again[i], 16)
                if c == 0 and i == 0:
                    dve.wait_ge(s_bce, 4)
                cs = slice(c * 512, (c + 1) * 512)
                y = bank[(5 * c + i) % 8][:, :]
                link(dve.tensor_mul(y, y, gate1[:, stream[i], cs]))
                dve.tensor_add(x1[:, i, cs], x1[:, i, cs], y).then_inc(s_mixe, 1)
            if c == 0:
                split_lo(N_MIX + 3, PIECE)
        dve_moe(dve, link)

    es.close()


INS = ["x_prompt", "x_sample", "cache_ckv", "cache_krope", "c", "c_ctx", "norm1", "w_ada", "b_ada", "w_in",
       "conv_w", "w_conv_out", "q_norm", "w_uq", "kv_norm", "w_ukv", "w_o", "w_mix_out", "norm2", "w_grp",
       "w_exp", "w_up", "w_gate", "w_down", "final_norm"]
OUTS = [("y_prompt", (1, N_PROMPT, D)), ("y_sample", (1, N_SAMPLE, D)),
        ("new_ckv", (1, 1, N_PROMPT, KVL)), ("new_krope", (1, 1, N_PROMPT, ROPE))]


def kernel(**inputs):
    import concourse.bacc as bacc
    from concourse.bass_utils import run_bass_kernel_spmd

    nc = bacc.Bacc("TRN2", target_bir_lowering=False, num_devices=1)
    arrays = {f"in_{name}": np.ascontiguousarray(inputs[name]) for name in INS}
    arrays["in_consts"] = constants()
    io = {name[3:]: nc.dram_tensor(name, a.shape, mybir.dt.from_np(a.dtype), kind="ExternalInput").ap()
          for name, a in arrays.items()}
    for name, shape in OUTS:
        io[name] = nc.dram_tensor(f"out_{name}", shape, F32, kind="ExternalOutput").ap()
    build(nc, io)
    r = run_bass_kernel_spmd(nc, [arrays], core_ids=[0])
    return tuple(r.results[0][f"out_{name}"] for name, _ in OUTS)
```

```python
from contextlib import ExitStack

import numpy as np

import concourse.bass as bass
from concourse import mybir

ALU = mybir.AluOpType
ACT = mybir.ActivationFunctionType
AXX = mybir.AxisListType.X
F32 = mybir.dt.float32
F32R = mybir.dt.float32r
BF16 = mybir.dt.bfloat16
U32 = mybir.dt.uint32
I32 = mybir.dt.int32

P = 128
D = 1024
KD = D // P
N_SAMPLE, N_PROMPT, N_PAST = 512, 128, 128
T = N_SAMPLE + N_PROMPT
NT = T // P
NTS = N_SAMPLE // P
HALF = T // 2
NH, NOPE, ROPE, VH = 8, 64, 32, 64
QK = NOPE + ROPE
QL, KVL = 256, 128
LAT = QL + KVL + ROPE
KEYS = N_SAMPLE + N_PAST
NKT = KEYS // P
ALLK = KEYS + N_PROMPT
SCALE = float(QK) ** -0.5
GRID_W = 64
NG, EPG = 4, 8
NE = NG * EPG
DE = 256
EPS = 1e-6
PIECE = 2048
C_BG, C_CG, C_U, C_LAT = 0, D, 2 * D, 3 * D
C_GC = C_LAT + LAT
C_GM = C_GC + D
FAR = 1 << 16
BIG = 1e30
X_MAX = 2 * ((2 * T // P - 1 + 1) // 2)
TILES = NE + X_MAX + 2

K_ID, K_TRI, K_ONE = 0, 128, 256
K_SEL = 384
K_COS, K_SIN = 640, 704
K_IOTA = 768
K_SLOT = K_IOTA + TILES
K_REV = K_SLOT + P
K_VAL = K_REV + NE
K_MULT = K_VAL + 4 * NT
K_EVEN = K_MULT + NT - 1
K_N = K_EVEN + X_MAX // 2


def constants():
    c = np.zeros((P, K_N), np.float32)
    c[:, K_ID:K_ID + P] = np.eye(P)
    c[:, K_TRI:K_TRI + P] = np.triu(np.ones((P, P)), 1)
    c[:, K_ONE:K_ONE + P] = 1
    for s in range(2):
        c[[s, 2 + s, 4], K_SEL + s * P:K_SEL + (s + 1) * P] = 1
    inv = 1.0 / (np.float32(10000.0) ** (np.arange(0, 16, 2, dtype=np.float32) / np.float32(16)))
    tok = np.arange(N_SAMPLE)
    ang = np.stack([(tok // GRID_W).astype(np.float32)[:, None] * inv,
                    (tok % GRID_W).astype(np.float32)[:, None] * inv], 1).astype(np.float32)
    for k, f in ((K_COS, np.cos), (K_SIN, np.sin)):
        c[:, k:k + 64] = f(ang).reshape(NTS, P, 16).transpose(1, 0, 2).reshape(P, 64)
    c[:, K_IOTA:K_IOTA + TILES] = np.arange(TILES)
    c[:, K_SLOT:K_SLOT + P] = np.arange(P)
    c[:, K_REV:K_REV + NE] = NE - np.arange(NE)
    t = np.arange(P)[:, None] + P * np.arange(NT)
    val = np.stack([np.stack([t, 2 * t + e], 2) for e in range(2)], 1)
    c[:, K_VAL:K_VAL + 4 * NT] = (val - FAR).reshape(P, 4 * NT)
    c[:, K_MULT:K_MULT + NT - 1] = P * np.arange(1, NT)
    c[:, K_EVEN:K_EVEN + X_MAX // 2] = np.arange(0, X_MAX, 2)
    return c


def build(nc, io):
    es = ExitStack()

    def sem(name):
        return es.enter_context(nc.semaphore(name))

    placed = []

    def sb(name, shape, dt=F32, scope=None):
        placed.append(int(np.prod(shape[1:])) * (2 if dt == BF16 else 4))
        return (scope or es).enter_context(nc.sbuf_tensor(name, shape, dt))

    H2D = nc.dram_tensor("h2_rows", [T, D], F32, kind="Internal").ap()
    YD = nc.dram_tensor("expert_rows", [2 * T, D], F32, kind="Internal").ap()
    MODD = nc.dram_tensor("mod_parts", [4, 6 * D], F32, kind="Internal").ap()
    MODS = nc.dram_tensor("mod_rows", [2, 4 * D], F32, kind="Internal").ap()

    cst = sb("cst", [P, K_N])
    ident = cst[:, K_ID:K_ID + P]
    vT = sb("vT", [P, 48])
    shsc = sb("shsc", [P, 16, 2])
    gain1 = sb("gain1", [P, KD, 2])
    stat = sb("stat", [P, 96])
    cond4 = sb("cond4", [P, KD, 4], F32R)
    stg = [sb(f"stg{i}", [4, 256]) for i in range(2)]
    extra_i = sb("extra_i", [P, 1], I32)
    expert_i = sb("expert_i", [P, TILES], I32)
    lists = sb("lists", [P, 2, TILES], U32)
    weights = sb("weights", [P, TILES])
    at_g = [sb(f"at_g{i}", [P, 1], U32) for i in range(2)]
    at_s = [sb(f"at_s{i}", [P, 1], U32) for i in range(2)]
    m_parts = sb("m_parts", [P, 4, 4 * D // P])
    m_bias = sb("m_bias", [P, 4 * D // P])
    tri_b = sb("tri_b", [P, P], BF16)
    one_b = sb("one_b", [P, P], BF16)

    mixer = ExitStack()
    raw = [sb(f"raw{i}", [P, PIECE], scope=mixer) for i in range(4)]
    hi = [sb(f"hi{i}", [P, PIECE], F32R, scope=mixer) for i in range(2)]
    lo = [sb(f"lo{i}", [P, PIECE], F32R, scope=mixer) for i in range(2)]
    hT = [sb(f"hT{i}", [P, KD, T], F32R, scope=mixer) for i in range(2)]
    RINGS = 8 * PIECE * 4 + 2 * KD * T * 4
    part0 = ExitStack()
    x_tok = sb("x_tok", [P, NT, D], scope=part0)
    xnT = sb("xnT", [P, KD, T], scope=part0)
    sq0 = sb("sq0", [P, D], scope=part0)
    mod1 = sb("mod1", [5, 2 * D], scope=part0)
    cond2 = sb("cond2", [P, KD, 2], scope=part0)
    vecs = sb("vecs", [48, P], scope=part0)
    part0.close()
    part1 = ExitStack()
    lat = sb("lat", [P, NT + 1, LAT], scope=part1)
    cqT = [sb(f"cqT{i}", [P, 2, T], F32R, scope=part1) for i in range(2)]
    ckvT = [sb(f"ckvT{i}", [P, ALLK], F32R, scope=part1) for i in range(2)]
    qtok = [sb(f"qtok{i}", [P, NH, QK], scope=part1) for i in range(2)]
    rt = [sb(f"rt{i}", [P, NH, 2, 8], scope=part1) for i in range(4)]
    part1.close()
    oT = [sb(f"oT{i}", [P, 4, T], F32R, scope=mixer) for i in range(2)]
    part2 = ExitStack()
    prob = [sb(f"prob{i}", [P, KEYS], scope=part2) for i in range(2)]
    pT = sb("pT", [P, NKT, N_SAMPLE], scope=part2)
    pT_p = sb("pT_p", [P, P], scope=part2)
    qT = sb("qT", [QK, NH, T], scope=part2)
    kT = sb("kT", [QK, NH, ALLK], scope=part2)
    V = sb("V", [P, NKT + 1, NH * VH], scope=part2)
    qn_b = sb("qn_b", [P, QL], scope=part2)
    kvn_b = sb("kvn_b", [P, KVL], scope=part2)
    part2.close()
    part3 = ExitStack()
    cT = [sb(f"cT{i}", [P, KD, T], F32R, scope=part3) for i in range(2)]
    part3c = ExitStack()
    cg_s = [sb(f"cg_s{i}", [P, T], scope=part3c) for i in range(2)]
    u = [sb(f"u{i}", [P, T + 4], scope=part3c) for i in range(2)]
    cv = [sb(f"cv{i}", [P, T + 2], scope=part3c) for i in range(2)]
    stg_c = sb("stg_c", [4, 4 * 256], scope=part3c)
    part3c.close()
    merged = sb("merged", [P, KD, T], scope=part3)
    sg = [sb(f"sg{i}", [P, T], scope=part3) for i in range(2)]
    part3.close()
    mixer.close()

    p6 = ExitStack()
    gain2 = sb("gain2", [P, 2, D], scope=p6)
    shift2 = sb("shift2", [P, 2, D], scope=p6)
    h2s = [sb(f"h2s{i}", [P, D], scope=p6) for i in range(2)]
    norm2_b = sb("norm2_b", [P, D], scope=p6)
    wrt = sb("wrt", [P, KD, NG + NE], scope=p6)
    slot_hot = sb("slot_hot", [P, 2 * NT, P], scope=p6)
    tile_val = sb("tile_val", [P, 2 * NT, 3, TILES], scope=p6)
    p6.close()
    placed.clear()
    xg = [sb(f"xg{i}", [P, D]) for i in range(2)]
    xgT = [[sb(f"xgT{i}{h}", [P, KD, P], F32R) for h in range(2)] for i in range(2)]
    yo = [sb(f"yo{i}", [P, D]) for i in range(2)]
    actT = [sb(f"actT{h}", [P, 2, P], F32R) for h in range(2)]
    sa = [sb(f"sa{i}", [P, DE]) for i in range(2)]
    act_v = [sb(f"act_v{i}", [P, DE]) for i in range(2)]
    behind_p6 = sb("behind_p6", [P, 512])
    lg36 = sb("lg36", [NG + NE, T])
    lg = sb("lg", [P, NT, NG + NE])
    hot = sb("hot", [P, 2, NT, NE])
    tile_hot = sb("tile_hot", [P, 2 * NT, TILES])
    mask = sb("mask", [P, NT, NE], BF16)
    r_t = sb("r_t", [P, 2, NT, NE])
    r_gs, r_ge, r_gh = (sb(f"r_g{i}", [P, NT, NG]) for i in range(3))
    r5 = [sb(f"r5_{i}", [P, NT]) for i in range(8)]
    r10 = [sb(f"r10_{i}", [P, 2, NT]) for i in range(6)]
    r_k = sb("r_k", [P, NE, NT - 1])
    r_x = [sb(f"r_x{i}", [P, NE]) for i in range(4)]
    r_e = sb("r_e", [P, X_MAX])
    val = sb("val", [P, 2, NT, 3])
    wh = [sb(f"wh{i}", [P, PIECE], F32R) for i in range(3)]
    wl = [sb(f"wl{i}", [P, PIECE], F32R) for i in range(3)]
    gate2 = sb("gate2", [P, 2, D])
    assert sum(placed) >= RINGS
    x1 = sb("x1", [P, NT, D])
    gate1 = sb("gate1", [P, 2, D])
    sq2 = sb("sq2", [P, D])
    p7 = ExitStack()
    wr = [[sb(f"wraw{k}{i}", [P, PIECE], scope=p7) for i in range(2)] for k in range(2)]
    early = ExitStack()
    h2T = sb("h2T", [P, KD, T], scope=early)
    early.close()
    wr += [[sb(f"wraw2{i}", [P, PIECE], scope=p7) for i in range(2)]]
    p7.close()
    p8 = ExitStack()
    ya = [sb(f"ya{i}", [P, 2, D], scope=p8) for i in range(NTS)]
    yt = [sb(f"yt{i}", [P, D], scope=p8) for i in range(2)]
    fn_b = sb("fn_b", [P, D], scope=p8)
    p8.close()

    pair = [es.enter_context(nc.psum_tensor(f"pair{i}", [P, 1024], F32)) for i in range(4)]
    bank = [pair[i // 2][:, i % 2 * 512:(i % 2 + 1) * 512] for i in range(8)]

    s_cst, s_vec, s_bc, s_cache, s_mod1, s_n2, s_fn = (sem(n) for n in (
        "cst_in", "vec_in", "norms_in", "cache_in", "mod1_in", "norm2_in", "fnorm_in"))
    s_parts, s_msum, s_mods, s_g1, s_sh2, s_g2 = (sem(n) for n in (
        "mod_parts_in", "mod_sum", "mod_rows_w", "gate1_in", "shift2_in", "gate2_in"))
    x_in = [sem(f"x_in{i}") for i in range(NT)]
    x_again = [sem(f"x_again{i}") for i in range(NT)]
    raw_in = [sem(f"raw_in{i}") for i in range(4)]
    hi_done, lo_done, piece_used = sem("hi_done"), sem("lo_done"), sem("piece_used")
    dchain, achain = sem("dve_chain"), sem("act_chain")
    s_ukv_v = sem("w_ukv_v_in")
    s_vT, c_vT, s_cond2, s_cond = sem("vT_ps"), sem("vT_sb"), sem("cond2"), sem("cond4_rdy")
    stg_ready = sem("stg_ready")
    mod_w = [sem(f"mod_w{i}") for i in range(2)]
    s_rms0, s_xn, s_xT, s_xTe = sem("rms0"), sem("xn"), sem("xT_ps"), sem("xT_sb")
    s_m1T, s_aff, s_hhi, s_hlo = sem("mod1T_ps"), sem("h_affine"), sem("h_hi"), sem("h_lo")
    s_lat, s_rmsl, s_latn, s_lT, s_lTh, s_lTe = (sem(n) for n in (
        "lat_ps", "rms_lat", "lat_norm", "latT_ps", "latT_hi", "latT_sb"))
    s_kr = sem("k_rope_sb")
    s_q, s_qr, s_tq, s_tqe, s_kv, s_kve = (sem(n) for n in (
        "q_ps", "q_roped", "qT_ps", "qT_sb", "kv_ps", "kv_sb"))
    s_sc, s_mx, s_ex, s_pn, s_tp, s_pe, s_pv, s_oh, s_ol = (sem(n) for n in (
        "scores", "neg_max", "exps", "probs", "pT_ps", "pT_sb", "pv", "o_hi", "o_lo"))
    blk_done, blk_free, mod_c = sem("conv_done"), sem("conv_free"), sem("mod_c")
    gate_done, gate_free, y_done, y_free = sem("gate_done"), sem("gate_free"), sem("y_done"), sem("y_free")
    s_mhi, s_mlo, s_mlo2 = sem("merged_hi"), sem("merged_lo"), sem("merged_lo_last")
    s_mix, s_mixe = sem("mix_ps"), sem("mix_sb")
    s_rms2, s_h2T, s_h2Te = sem("rms2"), sem("h2T_ps"), sem("h2T_sb")
    s_h2g, s_h2 = sem("h2_scaled"), sem("h2_tok")
    h2_w = [sem(f"h2_w{i}") for i in range(2)]
    s_wr, s_lg, s_lgT = sem("router_w_in"), sem("logits_ps"), sem("logitsT_ps")
    s_lge, s_lgTe = sem("logits_sb"), sem("logitsT_sb")
    s_gx, s_dx, s_mask, s_pos = sem("grp_exp"), sem("top2_exp"), sem("mask_rdy"), sem("pos_ps")
    s_tri, s_hots, s_lists, s_rdy = sem("tri_rdy"), sem("hots_rdy"), sem("lists_ps"), sem("lists_rdy")
    s_extra, s_gx_in, s_dx_in = (sem(n) for n in ("extra_rdy", "grp_shift", "top2_diff"))
    s_atg, s_ats = sem("at_g_rdy"), sem("at_s_rdy")
    s_latw = sem("lat_w")
    turns = {nc.sync: sem("sp_turns"), nc.gpsimd: sem("pool_turns"), nc.scalar: sem("act_turns")}

    w_done = [[sem(f"moe_{what}_{k}") for k in "abc"] for what in ("hi", "lo", "used")]
    wr_in = [[sem(f"moe_raw_{k}{i}") for i in range(2)] for k in "abc"]
    s_tr, s_xgh, s_xgl, s_si, s_act, s_at, s_aT, s_aTh, s_ya, s_yd, s_xg0 = (sem(n) for n in (
        "xgT_ps", "xgT_hi", "xgT_lo", "silu_up", "act_rdy", "actT_ps", "actT_sb", "actT_hi", "y_lower", "y_upper", "xg_zeroed"))
    gat, sct = ([sem(f"{n}{i}") for i in range(2)] for n in ("gathered", "scattered"))
    ya_in = [sem(f"ya_in{i}") for i in range(NT)]
    s_ysum = sem("expert_rows_added")
    y_out = [sem(f"y_out{i}") for i in range(2)]
    s_x2, s_sq3, s_rms3, s_yt = sem("x2_rdy"), sem("sq3"), sem("rms3"), sem("yt_rdy")

    def v3(t, k, c):
        return t[:, 0:k * c].rearrange("p (k c) -> p k c", k=k)

    def halves(p):
        return [bank[2 * p + h][:, 0:HALF] for h in range(2)]

    def both(p):
        return pair[p][:, :].rearrange("p (h c) -> p h c", h=2)[:, :, 0:HALF]

    w_in = io["w_in"][0]
    ID5 = cst[0:5, K_SEL:K_SEL + 2 * P]
    RQ, RKV, R2, R3 = 8, 16, 40, 56
    kcol = [0, 128, 256, 384, 640, 512]
    stream = [0, 0, 0, 0, 1]
    spans = [(0, N_SAMPLE, 0), (N_SAMPLE, T, 1)]
    POOL_LO = 5
    N_ADA1 = 8
    N_LAT, N_UQ, N_UKV, N_ATT, N_CONV, N_G, N_M, N_MIX = 8, 10, 11, 12, 24, 40, 48, 56
    units = [(h, i) for h in range(NH) for i in range(NT)]
    ada_first = [N_ATT + h + min(h, 4) for h in range(NH)]
    ada_second = [N_ATT + 2 * h + 1 for h in range(4)]

    def nth(j0, d):
        return j0 + (d + 1)

    def nth_dma(j0, d, each=16):
        return j0 * (each // 2) + (each // 2 * (d - d % 2) + each)

    A, B, C = range(3)

    def wait_alone(eng, sem_, value):
        eng.wait_ge(sem_, value)
        eng.sem_inc(turns[eng])

    def extra_of(eng):
        eng.wait_ge(s_extra, 1)
        return eng.value_load(extra_i[0:1, 0:1], min_val=0, max_val=X_MAX)

    def sp_moe(sp):
        def expert(ap, e, rows):
            return ap[0][bass.ds(e, 1), rows, :].rearrange("a (k p) c -> p (a k) c", p=P)

        def expert_of(j0, d):
            if isinstance(j0, int):
                return d
            return sp.value_load(expert_i[0:1, bass.ds(j0 + d, 1)], min_val=0, max_val=NE - 1)

        def mod_row(st, part):
            return MODS[st:st + 1, part * D:(part + 1) * D].partition_broadcast(P)

        def load_up(kind, j0, d):
            if not (isinstance(j0, int) and d < 2):
                wait_alone(sp, w_done[1][kind], nth(j0, d - 2))
            e = expert_of(j0, d)
            t = v3(wr[kind][d % 2], 4, 2 * DE)
            rows = slice(kind * 512, (kind + 1) * 512)
            sp.dma_start(t[:, :, 0:DE], expert(io["w_up"], e, rows)).then_inc(wr_in[kind][d % 2], 16)
            sp.dma_start(t[:, :, DE:], expert(io["w_gate"], e, rows)).then_inc(wr_in[kind][d % 2], 16)

        def load_down(j0, d):
            if not (isinstance(j0, int) and d < 2):
                wait_alone(sp, w_done[1][C], nth(j0, d - 2))
            e = expert_of(j0, d)
            sp.dma_start(v3(wr[C][d % 2], 2, D), expert(io["w_down"], e, slice(0, DE))).then_inc(wr_in[C][d % 2], 16)

        for j in range(2):
            load_up(A, 0, j)
            load_up(B, 0, j)
        sp.wait_ge(lo_done, N_MIX + 4)
        sp.dma_start(norm2_b[:, :], io["norm2"].partition_broadcast(P)).then_inc(s_n2, 16)
        for st in range(2):
            sp.dma_start(gain2[:, st, :], mod_row(st, 2)).then_inc(s_n2, 16)
        for st in range(2):
            sp.dma_start(shift2[:, st, :], mod_row(st, 1)).then_inc(s_sh2, 16)
        sp.dma_start(wrt[:, :, 0:NG], io["w_grp"][0].rearrange("(k p) c -> p k c", p=P)).then_inc(s_wr, 16)
        sp.dma_start(wrt[:, :, NG:], io["w_exp"][0].rearrange("(k p) c -> p k c", p=P)).then_inc(s_wr, 16)
        for i in range(NT):
            sp.wait_ge(s_h2, i + 1)
            sp.dma_start(H2D[i * P:(i + 1) * P, :], h2s[i % 2][:, :]).then_inc(h2_w[i % 2], 16)
        sp.wait_ge(s_lg, 2)
        load_down(0, 0)
        load_up(A, 0, 2)
        for st in range(2):
            sp.dma_start(gate2[:, st, :], mod_row(st, 3)).then_inc(s_g2, 16)
        X = extra_of(sp)
        with sp.Fori(2, X + NE, 2) as j0:
            for d in range(2):
                load_up(B, j0, d)
                load_down(j0, d - 1)
                load_up(A, j0, d + 1)
        load_down(X, NE - 1)
        wait_alone(sp, w_done[1][B], X + NE)
        wait_alone(sp, w_done[1][C], X + NE)
        wait_alone(sp, w_done[1][A], X + (NE + 1))
        sp.dma_start(fn_b[:, :], io["final_norm"].partition_broadcast(P)).then_inc(s_fn, 16)
        for p in range(2):
            sp.wait_ge(sct[p], X * 8 + NE * 8)
        for i in range(NT):
            if i >= NTS:
                sp.wait_ge(s_x2, i - NTS + 1)
            sp.dma_start(ya[i % NTS][:, :, :].rearrange("p a c -> p (a c)"),
                         YD[2 * i * P:2 * (i + 1) * P, :].rearrange("(p a) c -> p (a c)", a=2)
                         ).then_inc(ya_in[i], 16)
        for i in range(NT):
            store(sp, i)
        sp.wait_ge(y_out[0], 16 * 3)
        sp.wait_ge(y_out[1], 16 * 2)
        sp.wait_ge(s_latw, 32)

    def store(sp, i):
        sp.wait_ge(s_yt, i + 1)
        dst = io["y_sample"][0, i * P:(i + 1) * P, :] if i < NTS else io["y_prompt"][0]
        sp.dma_start(dst, yt[i % 2][:, :]).then_inc(y_out[i % 2], 16)

    def pool_moe(pool):
        pool.wait_ge(s_sh2, 32)
        for i in range(NT):
            pool.wait_ge(s_h2g, i + 1)
            pool.tensor_add(h2s[i % 2][:, :], h2s[i % 2][:, :], shift2[:, stream[i], :]).then_inc(s_h2, 1)

        def index(t, which, s_at, j0, d):
            pool.tensor_copy(t[d % 2][:, :], lists[:, which, bass.ds(j0 + d, 1)]).then_inc(s_at, 1)
            wait_alone(pool, s_at, nth(j0, d))

        def gather(j0, d):
            p = d % 2
            index(at_g, 0, s_atg, j0, d)
            pool.indirect_dma_start(
                out=xg[p][:, :], out_offset=None, in_=H2D,
                in_offset=bass.IndirectOffsetOnAxis(ap=at_g[p][:, :], axis=0),
                bounds_check=T - 1, oob_is_err=False).then_inc(gat[p], 16)

        def lo_down(j0, d):
            pool.wait_ge(w_done[0][C], nth(j0, d))
            pool.tensor_sub(wl[C][:, :], wr[C][d % 2][:, :], wh[C][:, :].bitcast(F32)).then_inc(w_done[1][C], 1)

        def scatter(j0, d):
            p = d % 2
            index(at_s, 1, s_ats, j0, d)
            pool.wait_ge(s_ya, nth(j0, d))
            wait_alone(pool, s_yd, nth(j0, d))
            pool.indirect_dma_start(
                out=YD, out_offset=bass.IndirectOffsetOnAxis(ap=at_s[p][:, :], axis=0),
                in_=yo[p][:, :], in_offset=None, bounds_check=2 * T - 1,
                oob_is_err=False).then_inc(sct[p], 16)

        def step(j0, d):
            first = isinstance(j0, int)
            if not (first and d < 1):
                pool.wait_ge(s_tr, nth(j0, d - 1))
                pool.wait_ge(gat[(d + 1) % 2], nth_dma(j0, d - 1))
            gather(j0, d + 1)
            if not (first and d < 2):
                if not (first and d < 4):
                    pool.wait_ge(sct[d % 2], nth_dma(j0, d - 4))
                scatter(j0, d - 2)
            if not (first and d < 2):
                lo_down(j0, d - 1)

        lo_down(0, 0)
        pool.wait_ge(s_rdy, 1)
        for i in range(2):
            pool.wait_ge(h2_w[i], 16 * (3 - i))
        pool.wait_ge(s_xg0, 2)
        gather(0, 0)
        for d in range(4):
            step(0, d)
        X = extra_of(pool)
        with pool.Fori(4, X + NE, 2) as j0:
            step(j0, 0)
            step(j0, 1)
        pool.wait_ge(sct[0], nth_dma(X, NE - 4))
        scatter(X, NE - 2)
        lo_down(X, NE - 1)
        pool.wait_ge(sct[1], nth_dma(X, NE - 3))
        scatter(X, NE - 1)
        pool.wait_ge(gat[0], nth_dma(X, NE))
        for p in range(2):
            pool.wait_ge(sct[p], X * 8 + NE * 8)
        for i in range(NT):
            pool.wait_ge(ya_in[i], 16)
            t = ya[i % NTS]
            pool.tensor_add(t[:, 0, :], t[:, 0, :], t[:, 1, :]).then_inc(s_ysum, 1)

    def pe_turn2(pe, i):
        pe.wait_ge(s_h2, i + 1)
        if i >= 2:
            pe.wait_ge(s_h2Te, i - 1)
        for k in range(KD):
            x = pe.transpose(bank[2 + 2 * (i % 2) + k // 4][:, (k % 4) * P:(k % 4 + 1) * P],
                             h2s[i % 2][:, k * P:(k + 1) * P], ident)
        x.then_inc(s_h2T, 1)

    def pe_logits(pe, i):
        pe.wait_ge(s_wr, 32)
        pe.wait_ge(s_h2Te, i + 1)
        o = bank[6 + i // NTS][0:NG + NE, (i % NTS) * P:(i % NTS + 1) * P]
        for k in range(KD):
            x = pe.matmul(o, wrt[:, k, :], h2T[:, k, i * P:(i + 1) * P], start=(k == 0), stop=(k == KD - 1))
        if i >= NTS - 1:
            x.then_inc(s_lg, 1)

    def pe_moe(pe):
        def prod(out, st, mv, first, last):
            pe.matmul(out, st[0], mv[0], start=first, stop=False)
            pe.matmul(out, st[0], mv[1], start=False, stop=False)
            return pe.matmul(out, st[1], mv[0], start=False, stop=last)

        pe_logits(pe, 0)
        for i in range(3, NT):
            pe_turn2(pe, i)
            pe_logits(pe, i - 2)
        for i in range(NT - 2, NT):
            pe_logits(pe, i)
        for i in range(NT):
            pe.wait_ge(s_lge, 1 if i < NTS else 2)
            x = pe.transpose(bank[0][:, i * 36:i * 36 + 36], lg36[:, i * P:(i + 1) * P], ident[0:36, 0:36])
        x.then_inc(s_lgT, 1)
        pe.wait_ge(s_mask, 1)
        pe.wait_ge(s_tri, 3)
        for i in range(NT):
            for j in range(i):
                pe.matmul(bank[1][:, i * NE:(i + 1) * NE], one_b[:, :], mask[:, j, :], start=(j == 0), stop=False)
            pe.matmul(bank[1][:, i * NE:(i + 1) * NE], tri_b[:, :], mask[:, i, :], start=(i == 0), stop=True)
        for j in range(NT):
            x = pe.matmul(bank[1][:, NT * NE:(NT + 1) * NE], one_b[:, :], mask[:, j, :], start=(j == 0),
                          stop=(j == NT - 1))
        x.then_inc(s_pos, 1)

        pe.wait_ge(s_hots, 1)
        for n in range(2 * NT):
            x = pe.matmul(bank[7][:, 0:3 * TILES], slot_hot[:, n, :],
                          tile_val[:, n, :, :].rearrange("p v t -> p (v t)"), start=(n == 0), stop=(n == 2 * NT - 1))
        x.then_inc(s_lists, 1)

        def turn(j0, d):
            first = isinstance(j0, int)
            pe.wait_ge(gat[d % 2], nth_dma(j0, d))
            if not (first and d < 1):
                pe.wait_ge(s_xgl, nth(j0, d - 1))
            for k in range(KD):
                x = pe.transpose(bank[k // 4][:, (k % 4) * P:(k % 4 + 1) * P],
                                 xg[d % 2][:, k * P:(k + 1) * P], ident)
            x.then_inc(s_tr, 1)

        def up(kind, j0, d):
            first = isinstance(j0, int)
            pe.wait_ge(w_done[1][kind], nth(j0, d))
            if kind == A:
                pe.wait_ge(s_xgl, nth(j0, d))
                if not (first and d < 2):
                    pe.wait_ge(s_act, nth(j0, d - 2))
            wv = [v3(t[kind], 4, 2 * DE) for t in (wh, wl)]
            for k in range(4):
                x = prod(bank[2 + d % 2][:, :], [t[:, 4 * kind + k, :] for t in xgT[d % 2]],
                         [t[:, k, :] for t in wv], kind == A and k == 0, kind == B and k == 3)
            x.then_inc(w_done[2][kind], 1)

        def act_turn(j0, d):
            pe.wait_ge(s_act, nth(j0, d))
            if not (isinstance(j0, int) and d < 1):
                pe.wait_ge(s_aT, nth(j0, d - 1))
            for f in range(2):
                x = pe.transpose(bank[4][:, f * P:(f + 1) * P], act_v[d % 2][:, f * P:(f + 1) * P], ident)
            x.then_inc(s_at, 1)

        def down(j0, d):
            pe.wait_ge(w_done[1][C], nth(j0, d))
            pe.wait_ge(s_aT, nth(j0, d))
            if not (isinstance(j0, int) and d < 1):
                pe.wait_ge(s_ya, nth(j0, d - 1))
                pe.wait_ge(s_yd, nth(j0, d - 1))
            wv = [v3(t[C], 2, D) for t in (wh, wl)]
            for c in range(2):
                for f in range(2):
                    x = prod(bank[5 + c][:, :], [t[:, f, :] for t in actT],
                             [t[:, f, c * 512:(c + 1) * 512] for t in wv], f == 0, f == 1)
            x.then_inc(w_done[2][C], 1)

        def step(j0, d):
            first = isinstance(j0, int)
            turn(j0, d)
            if not (first and d < 2):
                down(j0, d - 2)
            up(A, j0, d)
            if not (first and d < 1):
                act_turn(j0, d - 1)
            up(B, j0, d)

        step(0, 0)
        step(0, 1)
        X = extra_of(pe)
        with pe.Fori(2, X + NE, 2) as j0:
            step(j0, 0)
            step(j0, 1)
        down(X, NE - 2)
        act_turn(X, NE - 1)
        down(X, NE - 1)

    def act_moe(act, link):
        for i in range(NT):
            act.wait_ge(s_mixe, NT + i + 1)
            link(act.activation(sq2[:, :], x1[:, i, :], ACT.Square, accum_out=stat[:, R2 + i:R2 + i + 1]))
            act.activation(stat[:, R2 + 8 + i:R2 + 9 + i], stat[:, R2 + i:R2 + i + 1], ACT.Sqrt,
                           scale=1.0 / D, bias=stat[:, 95:96]).then_inc(s_rms2, 1)
            if i >= 2:
                h2T_out(act, i - 2)
        for i in range(NT - 2, NT):
            h2T_out(act, i)
        act.wait_ge(wr_in[A][0], 32)
        act.copy(wh[A][:, :], wr[A][0][:, :]).then_inc(w_done[0][A], 1)
        for c in range(2):
            act.wait_ge(s_lg, c + 1)
            cs = slice(0, N_SAMPLE) if c == 0 else slice(N_SAMPLE, T)
            act.copy(lg36[:, cs], bank[6 + c][0:NG + NE, 0:N_SAMPLE if c == 0 else N_PROMPT]).then_inc(s_lge, 1)
        act.wait_ge(s_gx_in, 1)
        act.activation(r_ge[:, :, :], r_gs[:, :, :], ACT.Exp).then_inc(s_gx, 1)
        act.wait_ge(wr_in[B][0], 32)
        act.copy(wh[B][:, :], wr[B][0][:, :]).then_inc(w_done[0][B], 1)
        act.wait_ge(s_dx_in, 1)
        act.activation(r5[4][:, :], r5[3][:, :], ACT.Exp).then_inc(s_dx, 1)
        act.wait_ge(wr_in[C][0], 16)
        act.copy(wh[C][:, :], wr[C][0][:, :]).then_inc(w_done[0][C], 1)

        def hi_of(kind, j0, d):
            act.wait_ge(wr_in[kind][d % 2], nth_dma(j0, d, 32 if kind < C else 16))
            if not (isinstance(j0, int) and d < 1):
                act.wait_ge(w_done[2][kind], nth(j0, d - 1))
            act.copy(wh[kind][:, :], wr[kind][d % 2][:, :]).then_inc(w_done[0][kind], 1)

        def silu(j0, d):
            act.wait_ge(w_done[2][B], nth(j0, d))
            if not (isinstance(j0, int) and d < 2):
                act.wait_ge(s_act, nth(j0, d - 2))
            act.activation(sa[d % 2][:, :], bank[2 + d % 2][:, DE:2 * DE], ACT.Silu).then_inc(s_si, 1)

        def xg_hi(j0, d):
            act.wait_ge(s_tr, nth(j0, d))
            for b in range(2):
                x = act.copy(xgT[d % 2][0][:, 4 * b:4 * b + 4, :], v3(bank[b], 4, P))
            x.then_inc(s_xgh, 1)

        def y_half(j0, d):
            if not (isinstance(j0, int) and d < 2):
                act.wait_ge(sct[d % 2], nth_dma(j0, d - 2))
            wait_alone(act, w_done[2][C], nth(j0, d))
            act.activation(yo[d % 2][:, 0:512], bank[5][:, :], ACT.Copy,
                           scale=weights[:, bass.ds(j0 + d, 1)]).then_inc(s_ya, 1)

        def step(j0, d):
            first = isinstance(j0, int)
            if not (first and d < 1):
                silu(j0, d - 1)
            xg_hi(j0, d)
            if not (first and d < 1):
                hi_of(B, j0, d)
            if not (first and d < 2):
                y_half(j0, d - 2)
                hi_of(C, j0, d - 1)
            hi_of(A, j0, d + 1)

        step(0, 0)
        step(0, 1)
        X = extra_of(act)
        with act.Fori(2, X + NE, 2) as j0:
            step(j0, 0)
            step(j0, 1)
        silu(X, NE - 1)
        y_half(X, NE - 2)
        hi_of(C, X, NE - 1)
        y_half(X, NE - 1)
        for i in range(NT):
            act.wait_ge(s_x2, i + 1)
            link(act.activation(sq2[:, :], x1[:, i, :], ACT.Square, accum_out=stat[:, R3 + i:R3 + i + 1]))
            act.activation(stat[:, R3 + 8 + i:R3 + 9 + i], stat[:, R3 + i:R3 + i + 1], ACT.Sqrt,
                           scale=1.0 / D, bias=stat[:, 95:96]).then_inc(s_rms3, 1)

    def h2T_out(act, i):
        act.wait_ge(s_h2T, i + 1)
        for b in range(2):
            x = act.copy(h2T[:, 4 * b:4 * b + 4, i * P:(i + 1) * P], v3(bank[2 + 2 * (i % 2) + b], 4, P))
        x.then_inc(s_h2Te, 1)

    def dve_moe(dve, link):
        dve.wait_ge(s_h2g, NT)
        for i in range(2):
            dve.memset(xg[i][:, :], 0.0).then_inc(s_xg0, 1)
        dve.tensor_copy(val[:, :, :, 0:2], cst[:, K_VAL:K_VAL + 4 * NT].rearrange("p (c t v) -> p c t v", c=2, v=2))

        def lo_of(kind, j0, d):
            dve.wait_ge(w_done[0][kind], nth(j0, d))
            dve.tensor_sub(wl[kind][:, :], wr[kind][d % 2][:, :], wh[kind][:, :].bitcast(F32)
                           ).then_inc(w_done[1][kind], 1)

        lo_of(A, 0, 0)
        dve.wait_ge(s_lgT, 1)
        link(dve.tensor_copy(lg[:, :, :], v3(bank[0], NT, NG + NE)))

        def wide(ap, n):
            return ap.unsqueeze(2).to_broadcast([P, NT, n])

        def pick(src, top, hot_, n):
            rev = cst[:, K_REV + NE - n:K_REV + NE].unsqueeze(1).to_broadcast([P, NT, n])
            t = r_t[:, 0, :, 0:n]
            link(dve.tensor_reduce(top, src, AXX, ALU.max))
            link(dve.tensor_tensor(hot_, src, wide(top, n), ALU.is_equal))
            link(dve.tensor_mul(t, hot_, rev))
            link(dve.tensor_reduce(r5[7][:, :], t, AXX, ALU.max))
            link(dve.tensor_tensor(hot_, t, wide(r5[7][:, :], n), ALU.is_equal))

        gl, el = lg[:, :, 0:NG], lg[:, :, NG:]
        pick(gl, r5[0][:, :], r_gh[:, :, :], NG)
        dve.tensor_tensor(r_gs[:, :, :], gl, wide(r5[0][:, :], NG), ALU.subtract).then_inc(s_gx_in, 1)
        link(dve.tensor_scalar(r_gh[:, :, :], r_gh[:, :, :], BIG, -BIG, ALU.mult, ALU.add))
        link(dve.tensor_add(el.rearrange("p t (g e) -> p t g e", g=NG), el.rearrange("p t (g e) -> p t g e", g=NG),
                            r_gh[:, :, :].unsqueeze(3).to_broadcast([P, NT, NG, EPG])))
        pick(el, r5[1][:, :], hot[:, 0], NE)
        link(dve.scalar_tensor_tensor(out=el, in0=hot[:, 0], scalar=-4 * BIG, in1=el, op0=ALU.mult, op1=ALU.add))
        pick(el, r5[2][:, :], hot[:, 1], NE)
        dve.tensor_add(mask[:, :, :], hot[:, 0], hot[:, 1]).then_inc(s_mask, 1)
        dve.tensor_sub(r5[3][:, :], r5[2][:, :], r5[1][:, :]).then_inc(s_dx_in, 1)

        def picked(dst, table):
            link(dve.tensor_mul(r_t[:, :, :, :], hot[:, :, :, :], table))
            link(dve.tensor_reduce(dst, r_t[:, :, :, :], AXX, ALU.add))

        def over(ap):
            return ap.unsqueeze(1).unsqueeze(1).to_broadcast([P, 2, NT, NE])

        iota = cst[:, K_IOTA:K_IOTA + NE]
        expert, place, move, beyond, tile, slot = (r[:, :, :] for r in r10)
        picked(expert, over(iota))
        dve.wait_ge(s_gx, 1)
        link(dve.tensor_reduce(r5[5][:, :], r_ge[:, :, :], AXX, ALU.add))
        dve.wait_ge(s_dx, 1)
        link(dve.tensor_scalar(r5[6][:, :], r5[4][:, :], 1.0, None, ALU.add))
        link(dve.tensor_mul(r5[6][:, :], r5[6][:, :], r5[5][:, :]))
        link(dve.reciprocal(val[:, 0, :, 2], r5[6][:, :]))
        link(dve.tensor_mul(val[:, 1, :, 2], val[:, 0, :, 2], r5[4][:, :]))
        dve.wait_ge(s_pos, 1)
        cnt = bank[1][:, NT * NE:(NT + 1) * NE]
        mult = cst[:, K_MULT:K_MULT + NT - 1]
        link(dve.tensor_tensor(r_k[:, :, :], cnt.unsqueeze(2).to_broadcast([P, NE, NT - 1]),
                               mult.unsqueeze(1).to_broadcast([P, NE, NT - 1]), ALU.is_gt))
        link(dve.tensor_reduce(r_x[0][:, :], r_k[:, :, :], AXX, ALU.add))
        a, b = 0, 1
        for sh in (1, 2, 4, 8, 16):
            dve.tensor_copy(r_x[b][:, 0:sh], r_x[a][:, 0:sh])
            link(dve.tensor_add(r_x[b][:, sh:], r_x[a][:, sh:], r_x[a][:, 0:NE - sh]))
            a, b = b, (a if sh > 1 else 2)
        incl, skip = r_x[a], r_x[3]
        link(dve.tensor_sub(skip[:, :], incl[:, :], r_x[0][:, :]))
        link(dve.scalar_tensor_tensor(out=skip[:, :], in0=skip[:, :], scalar=float(NE - 1), in1=iota,
                                      op0=ALU.add, op1=ALU.subtract))
        picked(place, bank[1][:, 0:NT * NE].rearrange("p (t e) -> p t e", t=NT).unsqueeze(1)
               .to_broadcast([P, 2, NT, NE]))
        k = r_k[:, 0:2 * NT, :]
        flat = place.rearrange("p c t -> p (c t)")
        link(dve.tensor_tensor(k, flat.unsqueeze(2).to_broadcast([P, 2 * NT, NT - 1]),
                               mult.unsqueeze(1).to_broadcast([P, 2 * NT, NT - 1]), ALU.is_ge))
        link(dve.tensor_reduce(beyond.rearrange("p c t -> p (c t)"), k, AXX, ALU.add))
        picked(move, over(skip[:, :]))
        dve.scalar_tensor_tensor(out=slot, in0=beyond, scalar=-float(P), in1=place, op0=ALU.mult, op1=ALU.add)
        link(dve.scalar_tensor_tensor(out=tile, in0=place, scalar=float(P), in1=move, op0=ALU.is_ge, op1=ALU.mult))
        link(dve.tensor_add(tile, tile, beyond))
        link(dve.tensor_add(tile, tile, expert))
        n2 = 2 * NT
        link(dve.tensor_tensor(tile_hot[:, :, :], tile.rearrange("p c t -> p (c t)").unsqueeze(2)
                               .to_broadcast([P, n2, TILES]),
                               cst[:, K_IOTA:K_IOTA + TILES].unsqueeze(1).to_broadcast([P, n2, TILES]),
                               ALU.is_equal))
        for v in range(3):
            dve.tensor_mul(tile_val[:, :, v, :], tile_hot[:, :, :],
                           val[:, :, :, v].rearrange("p c t -> p (c t)").unsqueeze(2).to_broadcast([P, n2, TILES]))
        dve.tensor_tensor(slot_hot[:, :, :], slot.rearrange("p c t -> p (c t)").unsqueeze(2)
                          .to_broadcast([P, n2, P]),
                          cst[:, K_SLOT:K_SLOT + P].unsqueeze(1).to_broadcast([P, n2, P]),
                          ALU.is_equal).then_inc(s_hots, 1)
        lo_of(B, 0, 0)
        dve.wait_ge(s_lists, 1)
        dve.tensor_scalar(lists[:, :, :], v3(bank[7], 2, TILES), float(FAR), None, ALU.add)
        dve.tensor_copy(weights[:, :], bank[7][:, 2 * TILES:3 * TILES]).then_inc(s_rdy, 1)
        dve.tensor_scalar(r5[7][:, 0:X_MAX // 2], cst[:, K_EVEN:K_EVEN + X_MAX // 2], incl[:, NE - 1:NE], 2.0,
                          ALU.is_lt, ALU.mult)
        by_q = r_t[:, :, :, :].rearrange("p c t e -> p (c t) e")[:, 0:X_MAX, :]
        link(dve.tensor_tensor(by_q, incl[:, :].unsqueeze(1).to_broadcast([P, X_MAX, NE]),
                               cst[:, K_IOTA:K_IOTA + X_MAX].unsqueeze(2).to_broadcast([P, X_MAX, NE]), ALU.is_le))
        dve.tensor_reduce(r5[6][:, 0:1], r5[7][:, 0:X_MAX // 2], AXX, ALU.add)
        link(dve.tensor_reduce(r_e[:, :], by_q, AXX, ALU.add))
        dve.tensor_copy(expert_i[:, 0:NE], iota)
        dve.memset(expert_i[:, NE + X_MAX:], 0)
        dve.tensor_copy(extra_i[:, :], r5[6][:, 0:1])
        dve.tensor_scalar(expert_i[:, NE:NE + X_MAX], r_e[:, :], float(NE - 1), None, ALU.min).then_inc(s_extra, 1)

        def gate_mul(j0, d):
            dve.wait_ge(s_si, nth(j0, d))
            if not (isinstance(j0, int) and d < 2):
                dve.wait_ge(s_at, nth(j0, d - 2))
            dve.tensor_mul(act_v[d % 2][:, :], bank[2 + d % 2][:, 0:DE], sa[d % 2][:, :]).then_inc(s_act, 1)

        def xg_lo(j0, d):
            dve.wait_ge(s_xgh, nth(j0, d))
            for b in range(2):
                x = dve.tensor_sub(xgT[d % 2][1][:, 4 * b:4 * b + 4, :], v3(bank[b], 4, P),
                                   xgT[d % 2][0][:, 4 * b:4 * b + 4, :].bitcast(F32))
            x.then_inc(s_xgl, 1)

        def act_out(j0, d):
            dve.wait_ge(s_at, nth(j0, d))
            if not (isinstance(j0, int) and d < 1):
                dve.wait_ge(w_done[2][C], nth(j0, d - 1))
            dve.tensor_copy(actT[0][:, :, :], v3(bank[4], 2, P)).then_inc(s_aTh, 1)
            dve.wait_ge(s_aTh, nth(j0, d))
            dve.tensor_sub(actT[1][:, :, :], v3(bank[4], 2, P), actT[0][:, :, :].bitcast(F32)).then_inc(s_aT, 1)

        def y_half(j0, d):
            dve.wait_ge(w_done[2][C], nth(j0, d))
            if not (isinstance(j0, int) and d < 2):
                dve.wait_ge(sct[d % 2], nth_dma(j0, d - 2))
            dve.tensor_scalar(yo[d % 2][:, 512:D], bank[6][:, :], weights[:, bass.ds(j0 + d, 1)], None,
                              ALU.mult).then_inc(s_yd, 1)

        def step(j0, d):
            first = isinstance(j0, int)
            if not (first and d < 1):
                gate_mul(j0, d - 1)
            xg_lo(j0, d)
            if not (first and d < 1):
                lo_of(B, j0, d)
            if not (first and d < 2):
                y_half(j0, d - 2)
            if not (first and d < 1):
                act_out(j0, d - 1)
            lo_of(A, j0, d + 1)

        step(0, 0)
        step(0, 1)
        X = extra_of(dve)
        with dve.Fori(2, X + NE, 2) as j0:
            step(j0, 0)
            step(j0, 1)
        gate_mul(X, NE - 1)
        y_half(X, NE - 2)
        act_out(X, NE - 1)
        y_half(X, NE - 1)
        dve.wait_ge(s_fn, 16)
        dve.wait_ge(s_g2, 32)
        for i in range(NT + 1):
            if i < NT:
                dve.wait_ge(s_ysum, i + 1)
                t = ya[i % NTS]
                link(dve.tensor_mul(t[:, 0, :], t[:, 0, :], gate2[:, stream[i], :]))
                dve.tensor_add(x1[:, i, :], x1[:, i, :], t[:, 0, :]).then_inc(s_x2, 1)
            if i >= 1:
                n = i - 1
                dve.wait_ge(s_rms3, n + 1)
                link(dve.reciprocal(stat[:, 72 + n:73 + n], stat[:, R3 + 8 + n:R3 + 9 + n]))
                if n >= 2:
                    dve.wait_ge(y_out[n % 2], 16 * (n // 2))
                dve.scalar_tensor_tensor(out=yt[n % 2][:, :], in0=x1[:, n, :], scalar=stat[:, 72 + n:73 + n],
                                         in1=fn_b[:, :], op0=ALU.mult, op1=ALU.mult).then_inc(s_yt, 1)

    block = es.enter_context(nc.Block())

    @block.sync
    def _(sp):
        sp.dma_start(cst[:, :], io["consts"]).then_inc(s_cst, 16)
        sp.dma_start(vecs[0:8, :], io["c"][0].rearrange("(k p) -> k p", p=P)).then_inc(s_vec, 16)
        sp.dma_start(vecs[8:16, :], io["c_ctx"].rearrange("(k p) -> k p", p=P)).then_inc(s_vec, 16)
        sp.dma_start(vecs[16:24, :], io["norm1"][0].rearrange("(k p) -> k p", p=P)).then_inc(s_vec, 16)
        sp.dma_start(vecs[24:48, :], io["conv_w"][0].rearrange("w (k p) -> (w k) p", p=P)).then_inc(s_vec, 16)

        def x_rows(i):
            return io["x_sample"][0, i * P:(i + 1) * P, :] if i < NTS else io["x_prompt"][0]

        for i in range(NT):
            sp.dma_start(x_tok[:, i, :], x_rows(i)).then_inc(x_in[i], 16)

        def load(n, src, k, c, i=0, step=0):
            if n >= 4:
                wait_alone(sp, lo_done, i * step + (n - 3))
            sp.dma_start(v3(raw[n % 4], k, c), src).then_inc(raw_in[n % 4], 16)

        def kpc(ap):
            return ap.rearrange("(k p) c -> p k c", p=P)

        def ada(n, c):
            load(n, kpc(io["w_ada"][0][:, c * 256:(c + 1) * 256]), KD, 256)

        for c in range(N_ADA1):
            ada(c, c)
        for kh in range(2):
            load(N_LAT + kh, kpc(w_in[kh * 512:(kh + 1) * 512, C_LAT:C_LAT + LAT]), 4, LAT)
        sp.dma_start(qn_b[:, :], io["q_norm"].partition_broadcast(P)).then_inc(s_bc, 16)
        sp.dma_start(kvn_b[:, :], io["kv_norm"].partition_broadcast(P)).then_inc(s_bc, 16)
        load(N_UQ, kpc(io["w_uq"][0]), 2, NH * QK)
        sp.wait_ge(lo_done, N_UKV - 3)
        for e, s_in in enumerate((raw_in[N_UKV % 4], s_ukv_v)):
            sp.dma_start(v3(raw[N_UKV % 4][:, e * 512:], NH, 64),
                         io["w_ukv"][0].rearrange("p (h s c) -> s p h c", s=2, h=NH)[e]).then_inc(s_in, 16)
        sp.wait_ge(s_hlo, KD)
        sp.dma_start(lat[:, NT, QL:QL + KVL], io["cache_ckv"][0, 0]).then_inc(s_cache, 16)
        sp.dma_start(lat[:, NT, QL + KVL:LAT], io["cache_krope"][0, 0]).then_inc(s_cache, 16)
        for n in range(N_ATT, N_CONV):
            ada(n, N_ADA1 + n - N_ATT)
        with sp.Fori(0, 4) as it:
            for q, c0 in enumerate((C_CG, C_U, C_BG)):
                load(N_CONV + q, kpc(w_in[:, bass.ds(it * 256 + c0, 256)]), KD, 256, it, 4)
            load(N_CONV + 3, kpc(io["w_ada"][0][:, bass.ds(it * 256 + 20 * 256, 256)]), KD, 256, it, 4)
        with sp.Fori(0, 2) as it:
            for mp in range(2):
                load(N_G + 2 * mp, kpc(w_in[:, bass.ds(it * 512 + (C_GC + mp * 256), 256)]), KD, 256, it, 4)
                load(N_G + 2 * mp + 1, kpc(io["w_conv_out"][0][:, bass.ds(it * 512 + mp * 256, 256)]),
                     KD, 256, it, 4)
        with sp.Fori(0, 2) as it:
            for mp in range(2):
                load(N_M + 2 * mp, kpc(w_in[:, bass.ds(it * 512 + (C_GM + mp * 256), 256)]), KD, 256, it, 4)
                load(N_M + 2 * mp + 1, kpc(io["w_o"][0][:, bass.ds(it * 512 + mp * 256, 256)]), 4, 256, it, 4)
        for c in range(2):
            for kh in range(2):
                load(N_MIX + 2 * c + kh,
                     kpc(io["w_mix_out"][0][kh * 512:(kh + 1) * 512, c * 512:(c + 1) * 512]), 4, 512)
        sp.wait_ge(s_mlo, POOL_LO)
        sp.wait_ge(s_mlo2, KD - POOL_LO)
        sp.wait_ge(s_mods, 16)
        for st in range(2):
            sp.dma_start(gate1[:, st, :], MODS[st:st + 1, 0:D].partition_broadcast(P)).then_inc(s_g1, 16)
        for i in range(NT):
            sp.dma_start(x1[:, i, :], x_rows(i)).then_inc(x_again[i], 16)

        sp_moe(sp)

    @block.gpsimd
    def _(pool):
        def mod_store(c):
            pool.wait_ge(stg_ready, c + 1)
            pool.dma_start(MODD[:, c * 256:(c + 1) * 256], stg[c % 2][:, :]).then_inc(mod_w[c % 2], 16)

        pool.dma_start(mod1[4:5, :], io["b_ada"][:, 0:2 * D]).then_inc(s_mod1, 16)
        pool.wait_ge(s_latn, NT)
        pool.dma_start(io["new_ckv"][0, 0], lat[:, NT - 1, QL:QL + KVL]).then_inc(s_latw, 16)
        pool.dma_start(io["new_krope"][0, 0], lat[:, NT - 1, QL + KVL:LAT]).then_inc(s_latw, 16)
        for c in range(N_ADA1, 20):
            n = N_ATT + c - N_ADA1
            if n + 1 in ada_second:
                pool.wait_ge(hi_done, n + 2)
                pool.tensor_sub(lo[(n + 1) % 2][:, :], raw[(n + 1) % 4][:, :],
                                hi[(n + 1) % 2][:, :].bitcast(F32)).then_inc(lo_done, 1)
            mod_store(c)
        for i in range(2):
            pool.wait_ge(mod_w[i], 16 * 6)
        pool.wait_ge(stg_ready, 24)
        pool.dma_start(MODD[:, 20 * 256:24 * 256], stg_c[:, :]).then_inc(mod_c, 16)
        pool.wait_ge(mod_c, 16)
        pool.dma_start(m_parts[:, :, :], MODD[:, 2 * D:6 * D].rearrange("r (p c) -> p r c", p=P)).then_inc(s_parts, 16)
        pool.dma_start(m_bias[:, :], io["b_ada"][0, 2 * D:6 * D].rearrange("(p c) -> p c", p=P)).then_inc(s_parts, 16)
        pool.wait_ge(s_parts, 32)
        mod2 = m_parts[:, 0:2, :]
        pool.tensor_add(mod2, mod2, m_parts[:, 2:4, :]).then_inc(s_msum, 1)
        pool.wait_ge(s_msum, 1)
        pool.tensor_add(mod2, mod2, m_bias[:, :].unsqueeze(1).to_broadcast([P, 2, 4 * D // P])).then_inc(s_msum, 1)
        pool.wait_ge(s_msum, 2)
        pool.dma_start(MODS.rearrange("s (p c) -> p s c", p=P), mod2).then_inc(s_mods, 16)
        for k in range(POOL_LO):
            pool.wait_ge(s_mhi, k + 1)
            pool.tensor_sub(hT[1][:, k, :], merged[:, k, :], hT[0][:, k, :].bitcast(F32)).then_inc(s_mlo, 1)
        pool_moe(pool)

    @block.tensor
    def _(pe):
        def prod(out, st, mv, first, last):
            pe.matmul(out, st[0], mv[0], start=first, stop=False)
            pe.matmul(out, st[0], mv[1], start=False, stop=False)
            return pe.matmul(out, st[1], mv[0], start=False, stop=last)

        def prod2(outs, st, mvs, first, last):
            for o, m in zip(outs, mvs):
                pe.matmul(o, st[0], m[0], start=first, stop=False)
            for o, m in zip(outs, mvs):
                pe.matmul(o, st[0], m[1], start=False, stop=False)
            for o, m in zip(outs, mvs):
                x = pe.matmul(o, st[1], m[0], start=False, stop=last)
            return x

        def ada(n, out, i=0, step=0):
            pe.wait_ge(lo_done, i * step + (n + 1))
            wh_, wl_ = v3(hi[n % 2], KD, 256), v3(lo[n % 2], KD, 256)
            def whole(k):
                return pe.matmul(out[0:4, :], cond4[:, k, :], wh_[:, k, :], start=(k == 0), stop=(k == KD - 1))

            x = whole(0)
            for k in range(KD):
                pe.matmul(out[0:2, :], cond4[:, k, 0:2], wl_[:, k, :], start=False, stop=False)
                if k:
                    x = whole(k)
            x.then_inc(piece_used, 1)

        pe.wait_ge(s_cst, 16)
        pe.wait_ge(s_vec, 64)
        pe.transpose(bank[7][:, 0:48], vecs[:, :], ident[0:48, 0:48]).then_inc(s_vT, 1)
        for i in range(NT):
            pe.wait_ge(s_xn, i + 1)
            if i >= 3:
                pe.wait_ge(s_xTe, i - 2)
            for k in range(KD):
                x = pe.transpose(bank[2 * (i % 3) + k // 4][:, (k % 4) * P:(k % 4 + 1) * P],
                                 x_tok[:, i, k * P:(k + 1) * P], ident)
            x.then_inc(s_xT, 1)
        def mod1_turn(c):
            pe.wait_ge(stg_ready, c + 1)
            for b in range(2 * c, 2 * c + 2):
                x = pe.matmul(bank[5][:, 2 * b:2 * b + 2], mod1[:, b * P:(b + 1) * P], ID5[:, 0:2 * P:P],
                              start=True, stop=True)
            return x

        pe.wait_ge(s_cond, 2)
        pe.wait_ge(c_vT, 1)
        pe.wait_ge(s_mod1, 16)
        pe.wait_ge(s_xTe, 3)
        for c in range(N_ADA1):
            if c >= 2:
                pe.wait_ge(stg_ready, c - 1)
            ada(c, bank[6 + c % 2][:, 0:256])
            if c >= 1:
                mod1_turn(c - 1)
        mod1_turn(N_ADA1 - 1).then_inc(s_m1T, 1)

        pe.wait_ge(s_xTe, NT)
        for kh in range(2):
            n = N_LAT + kh
            pe.wait_ge(lo_done, n + 1)
            wv = [v3(t, 4, LAT) for t in (hi[n % 2], lo[n % 2])]
            for i in range(NT):
                for k in range(4):
                    kk = 4 * kh + k
                    if i == 0:
                        pe.wait_ge(s_hlo, kk + 1)
                    x = prod(bank[i][:, 0:LAT], [t[:, kk, i * P:(i + 1) * P] for t in hT],
                             [t[:, k, :] for t in wv], kk == 0, kk == KD - 1)
                if i == NT - 1:
                    x.then_inc(piece_used, 1)
                elif kh == 1:
                    x.then_inc(s_lat, 1)
        pe.wait_ge(s_latn, NT)
        for i in range(NT + 1):
            b = bank[2 + i]
            if i == NT:
                pe.wait_ge(s_cache, 32)
            for k in range(2 if i < NT else 0):
                pe.transpose(b[:, k * P:(k + 1) * P], lat[:, i, k * P:(k + 1) * P], ident)
            pe.transpose(b[:, 256:384], lat[:, i, QL:QL + KVL], ident)
            pe.transpose(b[0:ROPE, 384:512], lat[:, i, QL + KVL:LAT], ident).then_inc(s_lT, 1)

        pe.wait_ge(lo_done, N_UQ + 1)
        wq = [v3(t, 2, NH * QK) for t in (hi[N_UQ % 2], lo[N_UQ % 2])]

        def q_of(i):
            pe.wait_ge(s_lTe, i + 1)
            if i == 1:
                pe.wait_ge(s_kr, 2)
            if i >= 2:
                pe.wait_ge(s_qr, i - 1)
            for c in range(2):
                for k in range(2):
                    x = prod(bank[2 * (i % 2) + c][:, 0:384], [t[:, k, i * P:(i + 1) * P] for t in cqT],
                             [t[:, k, c * 384:(c + 1) * 384] for t in wq], k == 0, k == 1)
            x.then_inc(s_q if i < NT - 1 else piece_used, 1)

        def q_turn(i):
            pe.wait_ge(s_qr, i + 1)
            if i < 2:
                pe.wait_ge(s_kr, 2 * i + 4)
            if i >= 2:
                pe.wait_ge(s_tqe, i - 1)
            for h in range(NH):
                x = pe.transpose(bank[4 + 2 * (i % 2) + h // 4][0:QK, (h % 4) * P:(h % 4 + 1) * P],
                                 qtok[i % 2][:, h, :], ident)
            x.then_inc(s_tq, 1)

        q_of(0)
        for i in range(NT):
            if i + 1 < NT:
                q_of(i + 1)
            q_turn(i)

        pe.wait_ge(lo_done, N_UKV + 1)
        pe.wait_ge(s_qr, NT)
        pe.wait_ge(s_lTe, NT + 1)
        wkv = (hi[N_UKV % 2], lo[N_UKV % 2])
        j = 0
        for hp in range(NH // 2):
            for c in range(2):
                if j >= 4:
                    pe.wait_ge(s_kve, j - 3)
                prod(bank[j % 4][:, 0:384], [t[:, hp * P:(hp + 1) * P] for t in wkv],
                     [t[:, c * 384:(c + 1) * 384] for t in ckvT], True, True).then_inc(s_kv, 1)
                j += 1
        for kt in range(NKT + 1):
            pe.wait_ge(s_kve, j - 3)
            prod(bank[j % 4][:, :], [t[:, kt * P:(kt + 1) * P] for t in ckvT],
                 [t[:, NH * NOPE:NH * P] for t in wkv], True, True).then_inc(s_kv if kt < NKT else piece_used, 1)
            j += 1

        def scores(n):
            h, i = units[n]
            if n >= 2:
                pe.wait_ge(s_ex, n - 1)
            qh = qT[:, h, i * P:(i + 1) * P]
            if i < NTS:
                for c in range(2):
                    x = pe.matmul(bank[2 * (n % 2) + c][:, 0:HALF], qh, kT[:, h, c * HALF:(c + 1) * HALF],
                                  start=True, stop=True)
            else:
                x = pe.matmul(bank[2 * (n % 2)][:, 0:P], qh, kT[:, h, KEYS:ALLK], start=True, stop=True)
            x.then_inc(s_sc, 1)

        def p_turn(n):
            h, i = units[n]
            pe.wait_ge(s_pn, n + 1)
            if n >= 1:
                pe.wait_ge(s_pe, n)
            for kt in range(NKT if i < NTS else 1):
                x = pe.transpose(bank[4 + kt // 4][:, (kt % 4) * P:(kt % 4 + 1) * P],
                                 prob[n % 2][:, kt * P:(kt + 1) * P], ident)
            x.then_inc(s_tp, 1)

        def pv_sample(h):
            pe.wait_ge(s_pe, h * NT + NTS)
            if h >= 1:
                pe.wait_ge(s_ol, 2 * h - 1)
            for kt in range(NKT):
                x = pe.matmul(bank[6][0:VH, :], V[:, kt, h * VH:(h + 1) * VH], pT[:, kt, :],
                              start=(kt == 0), stop=(kt == NKT - 1))
            x.then_inc(s_pv, 1)

        def pv_prompt(h):
            pe.wait_ge(s_pe, h * NT + NT)
            pe.wait_ge(stg_ready, N_ADA1 + h + 1 + min(h + 1, 4))
            if h >= 1:
                pe.wait_ge(s_ol, 2 * h)
            pe.matmul(bank[7][0:VH, 0:P], V[:, NKT, h * VH:(h + 1) * VH], pT_p[:, :],
                      start=True, stop=True).then_inc(s_pv, 1)

        def ada_att(n, h):
            pe.wait_ge(stg_ready, N_ADA1 + n - N_ATT)
            if h >= 1:
                pe.wait_ge(s_ol, 2 * h)
            ada(n, bank[7][:, 256:512])

        pe.wait_ge(s_kve, j)
        pe.wait_ge(s_tqe, NT)
        scores(0)
        scores(1)
        for n, (h, i) in enumerate(units):
            if n + 2 < len(units):
                scores(n + 2)
            p_turn(n)
            if i == 2:
                ada_att(ada_first[h], h)
            if i == NTS:
                pv_sample(h)
                if h < 4:
                    ada_att(ada_second[h], h)
            if i == 0 and h >= 1:
                pv_prompt(h - 1)
        pv_prompt(NH - 1)

        pe.wait_ge(s_ol, 2 * NH)
        with pe.Fori(0, 4) as it:
            q = 0
            for p in range(3):
                n = N_CONV + p
                pe.wait_ge(lo_done, it * 4 + (n + 1))
                wv = [v3(t, KD, 256) for t in (hi[n % 2], lo[n % 2])]
                for mm in range(2):
                    pe.wait_ge(blk_free, it * 6 + max(q - 3, 0) + 1)
                    if q == 2:
                        pe.wait_ge(stg_ready, it + 20)
                    for k in range(KD):
                        x = prod2(halves(q % 4), [t[:, k, mm * P:(mm + 1) * P] for t in wv],
                                  [[t[:, k, c * HALF:(c + 1) * HALF] for t in hT] for c in range(2)],
                                  k == 0, k == KD - 1)
                    x.then_inc(piece_used if mm else blk_done, 1)
                    q += 1
            pe.wait_ge(stg_ready, it + 20)
            pe.wait_ge(blk_free, it * 6 + 4)
            ada(N_CONV + 3, bank[4][:, 0:256], it, 4)

        pe.wait_ge(blk_free, 25)
        pe.wait_ge(stg_ready, 24)
        for n0, kd, mv, g in ((N_G, KD, cT, 0), (N_M, 4, oT, 1)):
            with pe.Fori(0, 2) as it:
                for mp in range(2):
                    for kind, (free, done, kk, rhs) in enumerate(((gate_free, gate_done, KD, hT),
                                                                  (y_free, y_done, kd, mv))):
                        n = n0 + 2 * mp + kind
                        pe.wait_ge(lo_done, it * 4 + (n + 1))
                        wv = [v3(t, kk, 256) for t in (hi[n % 2], lo[n % 2])]
                        for mm in range(2):
                            if g or mp:
                                pe.wait_ge(free, it * 4 + (8 * g + 2 * mp + mm))
                            else:
                                pe.wait_ge(free, it * (3 + mm) + 1)
                            for k in range(kk):
                                x = prod2(halves(2 * kind + mm), [t[:, k, mm * P:(mm + 1) * P] for t in wv],
                                          [[t[:, k, c * HALF:(c + 1) * HALF] for t in rhs] for c in range(2)],
                                          k == 0, k == kk - 1)
                            x.then_inc(piece_used if mm else done, 1)

        pe.wait_ge(y_free, 17)
        pe.wait_ge(gate_free, 17)
        for c in range(2):
            for kh in range(2):
                n = N_MIX + 2 * c + kh
                pe.wait_ge(lo_done, n + 1)
                wv = [v3(t, 4, 512) for t in (hi[n % 2], lo[n % 2])]
                for i in range(NT):
                    j = 5 * c + i
                    if kh == 0 and j >= 8:
                        pe.wait_ge(s_mixe, j - 7)
                    for k in range(4):
                        kk = 4 * kh + k
                        if c == 0 and i == 0:
                            if kk < POOL_LO:
                                pe.wait_ge(s_mlo, kk + 1)
                            else:
                                pe.wait_ge(s_mlo2, kk - POOL_LO + 1)
                        x = prod(bank[j % 8][:, :], [t[:, kk, i * P:(i + 1) * P] for t in hT],
                                 [t[:, k, :] for t in wv], kk == 0, kk == KD - 1)
                    if i == NT - 1:
                        x.then_inc(piece_used, 1)
                    elif kh == 1:
                        x.then_inc(s_mix, 1)
                    if c == 1 and kh == 1 and i >= 2:
                        pe_turn2(pe, i - 2)
        pe_moe(pe)

    @block.scalar
    def _(act):
        links = [0]

        def link(x):
            links[0] += 1
            x.then_inc(achain, 1)
            act.wait_ge(achain, links[0])

        def split_hi(n, size, i=0, step=0):
            act.wait_ge(raw_in[n % 4], i * (4 * step) + 16 * (n // 4 + 1))
            if n >= 2:
                act.wait_ge(piece_used, i * step + (n - 1))
            act.copy(hi[n % 2][:, 0:size], raw[n % 4][:, 0:size]).then_inc(hi_done, 1)

        act.wait_ge(c_vT, 1)
        act.activation(cond2[:, :, :].rearrange("p k s -> p s k"),
                       vT[:, 0:16].rearrange("p (s k) -> p s k", s=2), ACT.Silu).then_inc(s_cond2, 1)
        for i in range(NT):
            act.wait_ge(x_in[i], 16)
            link(act.activation(sq0[:, :], x_tok[:, i, :], ACT.Square, accum_out=stat[:, i:i + 1]))
        act.wait_ge(s_tri, 3)
        act.activation(stat[:, 0:NT], stat[:, 0:NT], ACT.Sqrt, scale=1.0 / D, bias=stat[:, 95:96]).then_inc(s_rms0, 1)
        split_hi(0, PIECE)
        split_hi(1, PIECE)
        for i in range(NT):
            act.wait_ge(s_xT, i + 1)
            for b in range(2):
                x = act.copy(xnT[:, 4 * b:4 * b + 4, i * P:(i + 1) * P],
                             v3(bank[2 * (i % 3) + b], 4, P))
            x.then_inc(s_xTe, 1)
        for n in range(2, N_LAT):
            split_hi(n, PIECE)
        for kh in range(2):
            split_hi(N_LAT + kh, 4 * LAT)
        for k in range(KD):
            act.wait_ge(s_aff, k + 1)
            act.copy(hT[0][:, k, :], xnT[:, k, :]).then_inc(s_hhi, 1)
        split_hi(N_UQ, 2 * NH * QK)
        for i in range(NT):
            act.wait_ge(s_lat, i + 1) if i < NT - 1 else act.wait_ge(piece_used, N_LAT + 2)
            if i == 0:
                act.wait_ge(s_hlo, KD)
            link(act.activation(qtok[0][:, 0:2, :].rearrange("p a b -> p (a b)")[:, 0:128], bank[i][:, 256:384],
                                ACT.Square, accum_out=stat[:, RKV + i:RKV + i + 1]))
            link(act.activation(qtok[0][:, 0:3, :].rearrange("p a b -> p (a b)")[:, 0:256], bank[i][:, 0:256],
                                ACT.Square, accum_out=stat[:, RQ + i:RQ + i + 1]))
        for r, n in ((RQ, QL), (RKV, KVL)):
            x = act.activation(stat[:, r:r + NT], stat[:, r:r + NT], ACT.Sqrt, scale=1.0 / n, bias=stat[:, 95:96])
        x.then_inc(s_rmsl, 1)
        act.wait_ge(s_ukv_v, 16)
        split_hi(N_UKV, NH * P)
        for i in range(NT + 1):
            b = bank[2 + i]
            act.wait_ge(s_lT, i + 1)
            if i < NT:
                act.copy(cqT[0][:, :, i * P:(i + 1) * P], v3(b, 2, P))
            act.copy(ckvT[0][:, kcol[i]:kcol[i] + P], b[:, 256:384]).then_inc(s_lTh, 1)
        for i in range(NT + 1):
            act.wait_ge(s_lTe, i + 1)
            act.copy(kT[NOPE:QK, :, kcol[i]:kcol[i] + P],
                     bank[2 + i][0:ROPE, 384:512].unsqueeze(1).to_broadcast([ROPE, NH, P])).then_inc(s_kr, 1)
        for i in range(NT):
            act.wait_ge(s_tq, i + 1)
            for b in range(2):
                x = act.copy(qT[:, 4 * b:4 * b + 4, i * P:(i + 1) * P], v3(bank[4 + 2 * (i % 2) + b], 4, P)[0:QK])
            x.then_inc(s_tqe, 1)
        j = 0
        for hp in range(NH // 2):
            for c in range(2):
                act.wait_ge(s_kv, j + 1)
                for e in range(2):
                    x = act.copy(kT[0:NOPE, 2 * hp + e, c * 384:(c + 1) * 384],
                                 bank[j % 4][e * 64:e * 64 + 64, 0:384])
                x.then_inc(s_kve, 1)
                j += 1
        for kt in range(NKT + 1):
            act.wait_ge(s_kv, j + 1) if kt < NKT else act.wait_ge(piece_used, N_UKV + 1)
            act.copy(V[:, kt, :], bank[j % 4][:, :]).then_inc(s_kve, 1)
            j += 1
        def exps(n):
            i, b = n % NT, n % 2
            st = 20 + 4 * b
            act.wait_ge(s_mx, n + 1)
            if n >= 2:
                act.wait_ge(s_tp, n - 1)
            if i < NTS:
                dst, src = prob[b][:, :].rearrange("p (h c) -> p h c", h=2), both(b)
            else:
                dst, src = prob[b][:, 0:P], bank[2 * b][:, 0:P]
            act.activation(dst, src, ACT.Exp, bias=stat[:, st:st + 1], scale=SCALE,
                           accum_out=stat[:, st + 1:st + 2]).then_inc(s_ex, 1)

        def o_hi(h, prompt):
            r = (h % 2) * 64
            act.wait_ge(s_pv, 2 * h + 1 + prompt)
            if prompt:
                x = act.copy(oT[0][r:r + 64, h // 2, N_SAMPLE:T], bank[7][0:VH, 0:P])
            else:
                x = act.copy(oT[0][r:r + 64, h // 2, 0:N_SAMPLE], bank[6][0:VH, :])
            x.then_inc(s_oh, 1)

        split_hi(N_ATT, PIECE)
        exps(0)
        for n, (h, i) in enumerate(units):
            if n + 1 < len(units):
                exps(n + 1)
            act.wait_ge(s_tp, n + 1)
            if i < NTS:
                if i == 0 and h >= 1:
                    act.wait_ge(s_pv, 2 * h - 1)
                act.copy(pT[:, :, i * P:(i + 1) * P], v3(pair[2], NKT, P)).then_inc(s_pe, 1)
            else:
                if h >= 1:
                    act.wait_ge(s_pv, 2 * h)
                act.copy(pT_p[:, :], bank[4][:, 0:P]).then_inc(s_pe, 1)
            if h >= 1 and i < 2:
                o_hi(h - 1, i)
            if i == 1 and h < 4:
                split_hi(ada_second[h], PIECE)
            if i == NTS and h + 1 < NH:
                split_hi(ada_first[h + 1], PIECE)
        for prompt in range(2):
            o_hi(NH - 1, prompt)
        for n in range(2):
            split_hi(N_CONV + n, PIECE)
        with act.Fori(0, 4) as it:
            for q in range(4):
                split_hi(N_CONV + 2 + q, PIECE, it, 4)
        act.sem_inc(gate_free)
        for n0, g in ((N_G, 0), (N_M, 1)):
            with act.Fori(0, 2) as it:
                for mp in range(2):
                    for mm in range(2):
                        jj = 8 * g + 2 * mp + mm
                        if mm:
                            act.wait_ge(piece_used, it * 4 + (n0 + 2 * mp + 1))
                        else:
                            act.wait_ge(gate_done, it * 2 + (4 * g + mp + 1))
                        if g or mp:
                            act.wait_ge(y_free, it * 4 + jj)
                        else:
                            act.wait_ge(y_free, it * (3 + mm) + 1)
                        for c, o in enumerate(halves(mm)):
                            x = act.activation(sg[mm][:, c * HALF:(c + 1) * HALF], o, ACT.Sigmoid)
                        x.then_inc(gate_free, 1)
                    split_hi(n0 + 2 * mp + 2, PIECE, it, 4)
                    split_hi(n0 + 2 * mp + 3, PIECE, it, 4)
        act.wait_ge(piece_used, N_M + 7)
        for k in range(KD):
            act.wait_ge(y_free, KD + k + 2)
            act.copy(hT[0][:, k, :], merged[:, k, :]).then_inc(s_mhi, 1)
        for k in range(2, 4):
            split_hi(N_MIX + k, PIECE)
        act_moe(act, link)

    @block.vector
    def _(dve):
        links = [0]
        base = [0, 0]

        def link(x):
            links[0] += 1
            x.then_inc(dchain, 1)
            dve.wait_ge(dchain, base[0] * base[1] + links[0] if base[1] else links[0])

        def split_lo(n, size, i=0, step=0):
            dve.wait_ge(hi_done, i * step + (n + 1))
            dve.tensor_sub(lo[n % 2][:, 0:size], raw[n % 4][:, 0:size],
                           hi[n % 2][:, 0:size].bitcast(F32)).then_inc(lo_done, 1)

        def ada_out(n, c, b):
            dve.wait_ge(piece_used, n + 1)
            if c < N_ADA1:
                dst = mod1[0:4, c * 256:(c + 1) * 256]
            else:
                dst = stg[c % 2][:, :]
                if c >= N_ADA1 + 2:
                    dve.wait_ge(mod_w[c % 2], 16 * ((c - N_ADA1) // 2))
            dve.tensor_copy(dst, b[0:4, :]).then_inc(stg_ready, 1)

        dve.memset(stat[:, 95:96], EPS).then_inc(s_tri, 1)
        dve.wait_ge(s_cst, 16)
        dve.tensor_copy(tri_b[:, :], cst[:, K_TRI:K_TRI + P]).then_inc(s_tri, 1)
        dve.tensor_copy(one_b[:, :], cst[:, K_ONE:K_ONE + P]).then_inc(s_tri, 1)
        dve.wait_ge(s_vT, 1)
        dve.tensor_copy(vT[:, :], bank[7][:, 0:48]).then_inc(c_vT, 1)
        dve.wait_ge(s_cond2, 1)
        dve.tensor_copy(cond4[:, :, 0:2], cond2[:, :, :]).then_inc(s_cond, 1)
        dve.wait_ge(s_cond, 1)
        dve.tensor_sub(cond4[:, :, 2:4], cond2[:, :, :], cond4[:, :, 0:2].bitcast(F32)).then_inc(s_cond, 1)
        dve.wait_ge(s_rms0, 1)
        link(dve.reciprocal(stat[:, 32:37], stat[:, 0:NT]))
        for i in range(NT):
            dve.tensor_scalar(x_tok[:, i, :], x_tok[:, i, :], stat[:, 32 + i:33 + i], None,
                              ALU.mult).then_inc(s_xn, 1)
        split_lo(0, PIECE)
        split_lo(1, PIECE)
        for c in range(N_ADA1):
            ada_out(c, c, bank[6 + c % 2][:, 0:256])
            split_lo(c + 2, PIECE if c + 2 < N_LAT else 4 * LAT)
        dve.wait_ge(s_m1T, 1)
        link(dve.tensor_copy(shsc[:, :, :], v3(bank[5], 16, 2)))
        link(dve.scalar_tensor_tensor(out=gain1[:, :, :], in0=shsc[:, 8:16, :], scalar=1.0,
                                      in1=vT[:, 16:24].unsqueeze(2).to_broadcast([P, KD, 2]),
                                      op0=ALU.add, op1=ALU.mult))
        dve.wait_ge(s_xTe, NT)

        def h_lo(k):
            dve.wait_ge(s_hhi, k + 1)
            dve.tensor_sub(hT[1][:, k, :], xnT[:, k, :], hT[0][:, k, :].bitcast(F32)).then_inc(s_hlo, 1)

        for k in range(KD):
            for a, z, s in spans:
                x = dve.tensor_scalar(xnT[:, k, a:z], xnT[:, k, a:z], gain1[:, k, s:s + 1], shsc[:, k, s:s + 1],
                                      ALU.mult, ALU.add)
            x.then_inc(s_aff, 1)
            if k:
                h_lo(k - 1)
        h_lo(KD - 1)

        def rope(dst, src, i, nh):
            cos, sin = (cst[:, k + 16 * i:k + 16 * i + 16].rearrange("p (a f) -> p a f", a=2)
                        .unsqueeze(1).to_broadcast([P, nh, 2, 8]) for k in (K_COS, K_SIN))
            for r, (half, tab) in enumerate(((0, cos), (1, sin), (1, cos), (0, sin))):
                x = dve.tensor_tensor(rt[r][:, 0:nh], src[:, :, :, half, :], tab, ALU.mult)
            link(x)
            dve.tensor_sub(dst[:, :, :, 0, :], rt[0][:, 0:nh], rt[1][:, 0:nh])
            return dve.tensor_add(dst[:, :, :, 1, :], rt[2][:, 0:nh], rt[3][:, 0:nh])

        def halfview(ap, nh):
            return ap.rearrange("p h (a b f) -> p h a b f", a=2, b=2)

        split_lo(N_UQ, 2 * NH * QK)
        dve.wait_ge(s_bc, 32)
        dve.wait_ge(s_rmsl, 1)
        dve.reciprocal(stat[:, 32:37], stat[:, RQ:RQ + NT])
        link(dve.reciprocal(stat[:, 37:42], stat[:, RKV:RKV + NT]))
        for i in range(NT):
            b = bank[i]
            dve.scalar_tensor_tensor(out=lat[:, i, 0:QL], in0=b[:, 0:QL], scalar=stat[:, 32 + i:33 + i],
                                     in1=qn_b[:, :], op0=ALU.mult, op1=ALU.mult)
            dve.scalar_tensor_tensor(out=lat[:, i, QL:QL + KVL], in0=b[:, QL:QL + KVL],
                                     scalar=stat[:, 37 + i:38 + i], in1=kvn_b[:, :], op0=ALU.mult, op1=ALU.mult)
            if i < NTS:
                x = rope(halfview(lat[:, i:i + 1, QL + KVL:LAT], 1),
                         halfview(b[:, QL + KVL:LAT].unsqueeze(1), 1), i, 1)
                link(x)
                dve.engine_nop().then_inc(s_latn, 1)
            else:
                dve.tensor_copy(lat[:, i, QL + KVL:LAT], b[:, QL + KVL:LAT]).then_inc(s_latn, 1)
        split_lo(N_UKV, NH * P)
        for i in range(NT + 1):
            b = bank[2 + i]
            dve.wait_ge(s_lTh, i + 1)
            if i < NT:
                dve.tensor_sub(cqT[1][:, :, i * P:(i + 1) * P], v3(b, 2, P),
                               cqT[0][:, :, i * P:(i + 1) * P].bitcast(F32))
            dve.tensor_sub(ckvT[1][:, kcol[i]:kcol[i] + P], b[:, 256:384],
                           ckvT[0][:, kcol[i]:kcol[i] + P].bitcast(F32)).then_inc(s_lTe, 1)
        for i in range(NT):
            dve.wait_ge(s_q, i + 1) if i < NT - 1 else dve.wait_ge(piece_used, N_UQ + 1)
            if i >= 2:
                dve.wait_ge(s_tq, i - 1)
            for c in range(2):
                src = v3(bank[2 * (i % 2) + c], 4, QK)
                dst = qtok[i % 2][:, 4 * c:4 * c + 4, :]
                if i < NTS:
                    dve.tensor_copy(dst[:, :, 0:NOPE], src[:, :, 0:NOPE])
                    x = rope(halfview(dst[:, :, NOPE:QK], 4), halfview(src[:, :, NOPE:QK], 4), i, 4)
                    link(x)
                else:
                    x = link(dve.tensor_copy(dst, src))
            dve.engine_nop().then_inc(s_qr, 1)
        def top(n):
            i, b = n % NT, n % 2
            dve.wait_ge(s_sc, n + 1)
            if i < NTS:
                link(dve.tensor_reduce(stat[:, 46 + b:47 + b], both(b), mybir.AxisListType.XY, ALU.max))
            else:
                link(dve.tensor_reduce(stat[:, 46 + b:47 + b], bank[2 * b][:, 0:P], AXX, ALU.max))
            dve.tensor_scalar(stat[:, 20 + 4 * b:21 + 4 * b], stat[:, 46 + b:47 + b], -SCALE, None,
                              ALU.mult).then_inc(s_mx, 1)

        def o_lo(h, prompt):
            r = (h % 2) * 64
            a, z = (N_SAMPLE, T) if prompt else (0, N_SAMPLE)
            dve.wait_ge(s_oh, 2 * h + 1 + prompt)
            dve.tensor_sub(oT[1][r:r + 64, h // 2, a:z], bank[6 + prompt][0:VH, 0:z - a],
                           oT[0][r:r + 64, h // 2, a:z].bitcast(F32)).then_inc(s_ol, 1)

        def ada_out_att(n):
            ada_out(n, N_ADA1 + n - N_ATT, bank[7][:, 256:512])

        split_lo(N_ATT, PIECE)
        top(0)
        top(1)
        for n, (h, i) in enumerate(units):
            b, w = n % 2, KEYS if i < NTS else P
            dve.wait_ge(s_ex, n + 1)
            link(dve.reciprocal(stat[:, 48 + b:49 + b], stat[:, 21 + 4 * b:22 + 4 * b]))
            dve.tensor_scalar(prob[b][:, 0:w], prob[b][:, 0:w], stat[:, 48 + b:49 + b], None,
                              ALU.mult).then_inc(s_pn, 1)
            if n + 2 < len(units):
                top(n + 2)
            if h >= 1 and 1 <= i < 3:
                o_lo(h - 1, i - 1)
            if i == 3:
                ada_out_att(ada_first[h])
            if i == NTS and h + 1 < NH:
                if h < 4:
                    dve.wait_ge(lo_done, ada_second[h] + 1)
                split_lo(ada_first[h + 1], PIECE)
            if i == 0 and 1 <= h <= 4:
                ada_out_att(ada_second[h - 1])
        for prompt in range(2):
            o_lo(NH - 1, prompt)
        for t in u:
            for a in (0, 513, 643):
                link(dve.memset(t[:, a:a + (2 if a == 513 else 1)], 0.0))
        dve.sem_inc(blk_free)
        dve.sem_inc(y_free)
        LINKS_CONV = 10
        for n in range(2):
            split_lo(N_CONV + n, PIECE)

        def freed(x, n):
            x.then_inc(blk_free, 1)
            dve.wait_ge(blk_free, it * 6 + (n + 1))

        def blk_wait(p, mm):
            if mm:
                dve.wait_ge(piece_used, it * 4 + (N_CONV + p + 1))
            else:
                dve.wait_ge(blk_done, it * 3 + (p + 1))

        with dve.Fori(0, 4) as it:
            base[:] = it, LINKS_CONV
            l0 = links[0]
            for mm in range(2):
                blk_wait(0, mm)
                for c, o in enumerate(halves(mm)):
                    x = dve.tensor_copy(cg_s[mm][:, c * HALF:(c + 1) * HALF], o)
                freed(x, mm + 1)
            split_lo(N_CONV + 2, PIECE, it, 4)
            for mm in range(2):
                blk_wait(1, mm)
                o = halves(2 + mm)
                dve.tensor_mul(u[mm][:, 1:1 + HALF], o[0], cg_s[mm][:, 0:HALF])
                dve.tensor_mul(u[mm][:, 1 + HALF:1 + N_SAMPLE], o[1][:, 0:N_SAMPLE - HALF],
                               cg_s[mm][:, HALF:N_SAMPLE])
                freed(dve.tensor_mul(u[mm][:, 3 + N_SAMPLE:3 + T], o[1][:, N_SAMPLE - HALF:HALF],
                                     cg_s[mm][:, N_SAMPLE:T]), mm + 3)
                W = T + 2
                cw = [vT[:, bass.ds(it * 2 + (24 + 8 * tap + mm), 1)] for tap in range(3)]
                link(dve.tensor_scalar(cv[mm][:, :], u[mm][:, 0:W], cw[0], None, ALU.mult))
                for tap in (1, 2):
                    link(dve.scalar_tensor_tensor(out=cv[mm][:, :], in0=u[mm][:, tap:tap + W], scalar=cw[tap],
                                                  in1=cv[mm][:, :], op0=ALU.mult, op1=ALU.add))
            split_lo(N_CONV + 3, PIECE, it, 4)
            for mm in range(2):
                blk_wait(2, mm)
                o = halves(mm)
                prod_ = cg_s[mm]
                dve.tensor_mul(prod_[:, 0:HALF], o[0], cv[mm][:, 0:HALF])
                dve.tensor_mul(prod_[:, HALF:N_SAMPLE], o[1][:, 0:N_SAMPLE - HALF], cv[mm][:, HALF:N_SAMPLE])
                link(dve.tensor_mul(prod_[:, N_SAMPLE:T], o[1][:, N_SAMPLE - HALF:HALF],
                                    cv[mm][:, N_SAMPLE + 2:T + 2]))
                c_hi, c_lo = (t[:, bass.ds(it * 2 + mm, 1), :].rearrange("p a t -> p (a t)") for t in cT)
                link(dve.tensor_copy(c_hi, prod_[:, :]))
                dve.tensor_sub(c_lo, prod_[:, :], c_hi.bitcast(F32)).then_inc(blk_free, 1)
            split_lo(N_CONV + 4, PIECE, it, 4)
            dve.wait_ge(piece_used, it * 4 + (N_CONV + 4))
            dve.tensor_copy(stg_c[:, bass.ds(it * 256, 256)], bank[4][0:4, 0:256]).then_inc(stg_ready, 1)
            split_lo(N_CONV + 5, PIECE, it, 4)
            assert links[0] - l0 == LINKS_CONV, links[0] - l0
        base[:] = 0, 0
        links[0] = l0 + 4 * LINKS_CONV
        dve.wait_ge(mod_c, 16)
        LINKS_GATE = 8
        for n0, g in ((N_G, 0), (N_M, 1)):
            with dve.Fori(0, 2) as it:
                base[:] = it, LINKS_GATE * g
                l0 = links[0]
                for mp in range(2):
                    split_lo(n0 + 2 * mp + 2, PIECE, it, 4)
                    for mm in range(2):
                        jj = 8 * g + 2 * mp + mm
                        if mm:
                            dve.wait_ge(piece_used, it * 4 + (n0 + 2 * mp + 2))
                        else:
                            dve.wait_ge(y_done, it * 2 + (4 * g + mp + 1))
                        dve.wait_ge(gate_free, it * 4 + (jj + 2))
                        m = merged[:, bass.ds(it * 4 + (2 * mp + mm), 1), :].rearrange("p a t -> p (a t)")
                        for c, o in enumerate(halves(2 + mm)):
                            cs = slice(c * HALF, (c + 1) * HALF)
                            if g:
                                x = dve.tensor_mul(sg[mm][:, cs], o, sg[mm][:, cs])
                                link(x)
                                x = dve.tensor_add(m[:, cs], m[:, cs], sg[mm][:, cs])
                            else:
                                x = dve.tensor_mul(m[:, cs], o, sg[mm][:, cs])
                        x.then_inc(y_free, 1)
                    split_lo(n0 + 2 * mp + 3, PIECE, it, 4)
                if g:
                    assert links[0] - l0 == LINKS_GATE, links[0] - l0
        base[:] = 0, 0
        links[0] = l0 + 2 * LINKS_GATE
        for k in range(POOL_LO, KD):
            dve.wait_ge(s_mhi, k + 1)
            dve.tensor_sub(hT[1][:, k, :], merged[:, k, :], hT[0][:, k, :].bitcast(F32)).then_inc(s_mlo2, 1)
        split_lo(N_MIX + 2, PIECE)

        def add_y(c, i):
            dve.wait_ge(s_mix, 4 * c + i + 1) if i < NT - 1 else dve.wait_ge(piece_used, N_MIX + 2 * c + 2)
            if c == 0:
                dve.wait_ge(x_again[i], 16)
            cs = slice(c * 512, (c + 1) * 512)
            y = bank[(5 * c + i) % 8][:, :]
            link(dve.tensor_mul(y, y, gate1[:, stream[i], cs]))
            dve.tensor_add(x1[:, i, cs], x1[:, i, cs], y).then_inc(s_mixe, 1)

        def scale_rows(i):
            dve.wait_ge(s_rms2, i + 1)
            link(dve.reciprocal(stat[:, 64 + i:65 + i], stat[:, R2 + 8 + i:R2 + 9 + i]))
            if i >= 2:
                dve.wait_ge(s_h2T, i - 1)
                dve.wait_ge(h2_w[i % 2], 16 * (i // 2))
            dve.scalar_tensor_tensor(out=h2s[i % 2][:, :], in0=x1[:, i, :], scalar=stat[:, 64 + i:65 + i],
                                     in1=gain2[:, stream[i], :], op0=ALU.mult, op1=ALU.mult).then_inc(s_h2g, 1)

        dve.wait_ge(s_g1, 32)
        for i in range(NT):
            add_y(0, i)
        split_lo(N_MIX + 3, PIECE)
        dve.wait_ge(s_n2, 48)
        link(dve.scalar_tensor_tensor(out=gain2[:, :, :], in0=gain2[:, :, :], scalar=1.0,
                                      in1=norm2_b[:, :].unsqueeze(1).to_broadcast([P, 2, D]),
                                      op0=ALU.add, op1=ALU.mult))
        for i in range(NT):
            add_y(1, i)
            if i >= 1:
                scale_rows(i - 1)
        scale_rows(NT - 1)
        dve_moe(dve, link)

    es.close()


INS = ["x_prompt", "x_sample", "cache_ckv", "cache_krope", "c", "c_ctx", "norm1", "w_ada", "b_ada", "w_in",
       "conv_w", "w_conv_out", "q_norm", "w_uq", "kv_norm", "w_ukv", "w_o", "w_mix_out", "norm2", "w_grp",
       "w_exp", "w_up", "w_gate", "w_down", "final_norm"]
OUTS = [("y_prompt", (1, N_PROMPT, D)), ("y_sample", (1, N_SAMPLE, D)),
        ("new_ckv", (1, 1, N_PROMPT, KVL)), ("new_krope", (1, 1, N_PROMPT, ROPE))]


def kernel(**inputs):
    import concourse.bacc as bacc
    from concourse.bass_utils import run_bass_kernel_spmd

    nc = bacc.Bacc("TRN2", target_bir_lowering=False, num_devices=1)
    arrays = {f"in_{name}": np.ascontiguousarray(inputs[name]) for name in INS}
    arrays["in_consts"] = constants()
    io = {name[3:]: nc.dram_tensor(name, a.shape, mybir.dt.from_np(a.dtype), kind="ExternalInput").ap()
          for name, a in arrays.items()}
    for name, shape in OUTS:
        io[name] = nc.dram_tensor(f"out_{name}", shape, F32, kind="ExternalOutput").ap()
    build(nc, io)
    r = run_bass_kernel_spmd(nc, [arrays], core_ids=[0])
    return tuple(r.results[0][f"out_{name}"] for name, _ in OUTS)
```
